# Optimizing a Trainium2 kernel written in Bass

```python
import jax, jax.numpy as jnp
from jax import lax
import numpy as np
import math

D_MODEL = 1024
BATCH = 1
SEQ = 512
DEPTH = 2

N_META = 16
CHUNK = 64
EPS = 1e-6

HG_HEADS = 4
HG_DIM = 128
HG_WIDTH = HG_HEADS * HG_DIM
RET_HEADS = 4
RET_DK = 32
RET_DV = 64
RET_QK_WIDTH = RET_HEADS * RET_DK
RET_V_WIDTH = RET_HEADS * RET_DV
ROPE_BASE = 10000.0
LRU_WIDTH = 256
LRU_BLOCKS = 4
LRU_BLOCK = LRU_WIDTH // LRU_BLOCKS
LRU_CONV = 4
LRU_C = 8.0
D_MIX = HG_WIDTH + RET_V_WIDTH + LRU_WIDTH
IN_SIZES = (HG_WIDTH, HG_WIDTH, HG_WIDTH, HG_WIDTH,
            RET_QK_WIDTH, RET_QK_WIDTH, RET_V_WIDTH, RET_V_WIDTH,
            LRU_WIDTH, LRU_WIDTH)
IN_COLS = sum(IN_SIZES)
IN_SPLITS = tuple(int(s) for s in np.cumsum(IN_SIZES)[:-1])
D_FF = 2816
FFN_CONV = 3


def rmsnorm(x, g):
    xf = x.astype(jnp.float32)
    y = xf * lax.rsqrt(jnp.mean(xf * xf, axis=-1, keepdims=True) + EPS)
    return (y * g.astype(jnp.float32)).astype(x.dtype)

def head_groupnorm(o, g):
    of = o.astype(jnp.float32)
    mu = jnp.mean(of, axis=-1, keepdims=True)
    var = jnp.mean(jnp.square(of - mu), axis=-1, keepdims=True)
    return ((of - mu) * lax.rsqrt(var + EPS) * g.astype(jnp.float32)).astype(o.dtype)

def causal_dwconv(x, w, b):
    width, ch = w.shape
    y = lax.conv_general_dilated(
        x, w[:, None, :].astype(x.dtype), window_strides=(1,), padding=[(width - 1, 0)],
        dimension_numbers=('NWC', 'WIO', 'NWC'), feature_group_count=ch)
    return y + b.astype(x.dtype)

def split_heads(a, n):
    bsz, t, _ = a.shape
    return a.reshape(bsz, t, n, -1).transpose(0, 2, 1, 3)

def merge_heads(a):
    bsz, h, t, d = a.shape
    return a.transpose(0, 2, 1, 3).reshape(bsz, t, h * d)

def to_chunks(a, pad):
    bsz, h, _, d = a.shape
    a = jnp.pad(a, ((0, 0), (0, 0), (pad, 0), (0, 0)))
    return a.reshape(bsz, h, -1, CHUNK, d).transpose(2, 0, 1, 3, 4)

def from_chunks(o, pad):
    n, bsz, h, c, d = o.shape
    return o.transpose(1, 2, 0, 3, 4).reshape(bsz, h, n * c, d)[:, :, pad:]

def hgrn2_chunked(q, k, v, log_f):
    bsz, h, t, dk = q.shape
    dv = v.shape[-1]
    pad = (-t) % CHUNK
    qc, kc, vc, gc = (to_chunks(a, pad) for a in (q, k, v, log_f))
    causal = jnp.tril(jnp.ones((CHUNK, CHUNK), dtype=bool))[:, :, None]

    def step(state, inp):
        qi, ki, vi, gi = inp
        b = jnp.cumsum(gi.astype(jnp.float32), axis=-2)
        diff = b[:, :, :, None, :] - b[:, :, None, :, :]
        decay = jnp.exp(jnp.where(causal, diff, -jnp.inf))
        scores = jnp.einsum('bhtd,bhtsd,bhsd->bhts', qi, decay, ki)
        o = jnp.einsum('bhts,bhse->bhte', scores, vi) + \
            jnp.einsum('bhtd,bhde->bhte', qi * jnp.exp(b), state)
        b_last = b[:, :, -1:, :]
        state = jnp.exp(b_last[:, :, 0, :])[..., None] * state + \
            jnp.einsum('bhsd,bhse->bhde', ki * jnp.exp(b_last - b), vi)
        return state, o

    s0 = jnp.zeros((bsz, h, dk, dv), jnp.float32)
    _, o = lax.scan(step, s0, (qc, kc, vc, gc))
    return from_chunks(o, pad)

def retention_chunked(q, k, v, log_gamma):
    bsz, h, t, dk = q.shape
    dv = v.shape[-1]
    pad = (-t) % CHUNK
    qc, kc, vc = (to_chunks(a, pad).transpose(1, 2, 0, 3, 4) for a in (q, k, v))
    idx = jnp.arange(CHUNK, dtype=jnp.float32)
    lg = log_gamma[:, None]
    rel = idx[:, None] - idx[None, :]
    dmat = jnp.where(rel >= 0, jnp.exp(lg[:, :, None] * jnp.maximum(rel, 0.0)), 0.0)
    scores = jnp.einsum('bhntd,bhnsd->bhnts', qc, kc) * dmat[None, :, None]
    intra = jnp.einsum('bhnts,bhnse->bhnte', scores, vc)
    w_state = jnp.exp(lg * (CHUNK - 1 - idx))
    kv = jnp.einsum('bhnsd,bhnse->nbhde', kc * w_state[None, :, None, :, None], vc)
    chunk_decay = jnp.exp(log_gamma * CHUNK)[None, :, None, None]

    def step(state, kv_n):
        return chunk_decay * state + kv_n, state

    _, r_prev = lax.scan(step, jnp.zeros((bsz, h, dk, dv), jnp.float32), kv)
    w_q = jnp.exp(lg * (idx + 1.0))
    inter = jnp.einsum('bhntd,nbhde->bhnte', qc * w_q[None, :, None, :, None], r_prev)
    o = (intra + inter).transpose(2, 0, 1, 3, 4)
    return from_chunks(o, pad)

def rope(x, cos, sin):
    x1, x2 = jnp.split(x, 2, axis=-1)
    return jnp.concatenate([x1 * cos - x2 * sin, x1 * sin + x2 * cos], axis=-1)

def rg_lru(x, gate_a_w, gate_a_b, gate_i_w, gate_i_b, lam):
    bsz, t, w = x.shape
    xb = x.reshape(bsz, t, LRU_BLOCKS, LRU_BLOCK)
    r = jax.nn.sigmoid(jnp.einsum('btnd,nde->btne', xb, gate_a_w).reshape(bsz, t, w) + gate_a_b)
    i = jax.nn.sigmoid(jnp.einsum('btnd,nde->btne', xb, gate_i_w).reshape(bsz, t, w) + gate_i_b)
    log_a = -LRU_C * r.astype(jnp.float32) * jax.nn.softplus(-lam.astype(jnp.float32))
    a = jnp.exp(log_a)
    u = jnp.sqrt(-jnp.expm1(2.0 * log_a)) * (i * x)

    def combine(c1, c2):
        a1, b1 = c1
        a2, b2 = c2
        return a1 * a2, a2 * b1 + b2

    _, hseq = lax.associative_scan(combine, (a, u), axis=1)
    return hseq.astype(x.dtype)

def hybrid_mixer(h, w_in, lb, hg_norm_g, ret_norm_g, lru_conv_w, lru_conv_b,
                 gate_a_w, gate_a_b, gate_i_w, gate_i_b, lru_lambda, w_out, cos, sin):
    proj = jnp.einsum('btd,dc->btc', h, w_in)
    hq, hf, hi, hg, rq, rk, rv, rg, lx, ly = jnp.split(proj, IN_SPLITS, axis=-1)

    z = hf.astype(jnp.float32)
    log_f = jnp.logaddexp(jnp.log(lb), jnp.log1p(-lb) + jax.nn.log_sigmoid(z))
    k_hg = (1.0 - lb) * jax.nn.sigmoid(-z)
    q_hg = jax.nn.silu(hq) * HG_DIM ** -0.5
    o_hg = hgrn2_chunked(split_heads(q_hg, HG_HEADS), split_heads(k_hg, HG_HEADS),
                         split_heads(hi, HG_HEADS), split_heads(log_f, HG_HEADS))
    o_hg = merge_heads(rmsnorm(o_hg, hg_norm_g)) * jax.nn.silu(hg)

    log_gamma = jnp.log1p(-jnp.exp2(-5.0 - jnp.arange(RET_HEADS, dtype=jnp.float32)))
    q_r = rope(split_heads(rq, RET_HEADS), cos, sin)
    k_r = rope(split_heads(rk, RET_HEADS), cos, sin) * RET_DK ** -0.5
    o_ret = retention_chunked(q_r, k_r, split_heads(rv, RET_HEADS), log_gamma)
    o_ret = merge_heads(head_groupnorm(o_ret, ret_norm_g)) * jax.nn.silu(rg)

    xc = causal_dwconv(lx, lru_conv_w, lru_conv_b)
    o_lru = rg_lru(xc, gate_a_w, gate_a_b, gate_i_w, gate_i_b, lru_lambda) * jax.nn.gelu(ly)

    merged = jnp.concatenate([o_hg, o_ret, o_lru], axis=-1)
    return jnp.einsum('btc,cd->btd', merged, w_out)

def conv_glu_ffn(h, w_up, conv_w, conv_b, w_down):
    u = causal_dwconv(jnp.einsum('btd,df->btf', h, w_up), conv_w, conv_b)
    gate, val = jnp.split(u, 2, axis=-1)
    return jnp.einsum('btf,fd->btd', jax.nn.silu(gate) * val, w_down)

def first_inputs(seed: int = 0) -> dict:
    key = jax.random.key(seed)
    ks = jax.random.split(key, 24)
    f32 = jnp.float32

    def nrm(k, shape, scale):
        return scale * jax.random.normal(k, shape, f32)

    a_c = jax.random.uniform(ks[10], (DEPTH, LRU_WIDTH), f32, 0.9, 0.999)
    s = a_c ** (1.0 / LRU_C)
    return {
        "x": nrm(ks[0], (BATCH, SEQ, D_MODEL), 1.0),
        "meta_tokens": nrm(ks[1], (N_META, D_MODEL), 1.0),
        "norm_mix_g": 1.0 + nrm(ks[2], (DEPTH, D_MODEL), 0.02),
        "w_in": nrm(ks[3], (DEPTH, D_MODEL, IN_COLS), D_MODEL ** -0.5),
        "hg_lb_logits": nrm(ks[4], (DEPTH, HG_WIDTH), 0.1),
        "hg_norm_g": 1.0 + nrm(ks[5], (DEPTH, HG_DIM), 0.02),
        "ret_norm_g": 1.0 + nrm(ks[6], (DEPTH, RET_DV), 0.02),
        "lru_conv_w": nrm(ks[7], (DEPTH, LRU_CONV, LRU_WIDTH), LRU_CONV ** -0.5),
        "lru_conv_b": nrm(ks[8], (DEPTH, LRU_WIDTH), 0.01),
        "lru_gate_a_w": nrm(ks[9], (DEPTH, LRU_BLOCKS, LRU_BLOCK, LRU_BLOCK), LRU_BLOCK ** -0.5),
        "lru_gate_a_b": nrm(ks[11], (DEPTH, LRU_WIDTH), 0.01),
        "lru_gate_i_w": nrm(ks[12], (DEPTH, LRU_BLOCKS, LRU_BLOCK, LRU_BLOCK), LRU_BLOCK ** -0.5),
        "lru_gate_i_b": nrm(ks[13], (DEPTH, LRU_WIDTH), 0.01),
        "lru_lambda": jnp.log(s) - jnp.log1p(-s),
        "w_out": nrm(ks[14], (DEPTH, D_MIX, D_MODEL), D_MIX ** -0.5),
        "norm_ffn_g": 1.0 + nrm(ks[15], (DEPTH, D_MODEL), 0.02),
        "ffn_w_up": nrm(ks[16], (DEPTH, D_MODEL, 2 * D_FF), D_MODEL ** -0.5),
        "ffn_conv_w": nrm(ks[17], (DEPTH, FFN_CONV, 2 * D_FF), FFN_CONV ** -0.5),
        "ffn_conv_b": nrm(ks[18], (DEPTH, 2 * D_FF), 0.01),
        "ffn_w_down": nrm(ks[19], (DEPTH, D_FF, D_MODEL), D_FF ** -0.5),
        "final_norm_g": 1.0 + nrm(ks[20], (D_MODEL,), 0.02),
    }

def first_block(x, meta_tokens, norm_mix_g, w_in, hg_lb_logits, hg_norm_g, ret_norm_g,
              lru_conv_w, lru_conv_b, lru_gate_a_w, lru_gate_a_b, lru_gate_i_w, lru_gate_i_b,
              lru_lambda, w_out, norm_ffn_g, ffn_w_up, ffn_conv_w, ffn_conv_b, ffn_w_down,
              final_norm_g):
    bsz = x.shape[0]
    meta = jnp.broadcast_to(meta_tokens[None].astype(x.dtype), (bsz, N_META, x.shape[-1]))
    h = jnp.concatenate([meta, x], axis=1)
    t = h.shape[1]

    pos = jnp.arange(t, dtype=jnp.float32)
    theta = ROPE_BASE ** (-jnp.linspace(0.0, 1.0, RET_DK // 2, dtype=jnp.float32))
    ang = pos[:, None] * theta[None, :]
    cos, sin = jnp.cos(ang), jnp.sin(ang)

    lb_all = jnp.cumsum(jax.nn.softmax(hg_lb_logits.astype(jnp.float32), axis=0), axis=0)
    lb_all = lb_all - lb_all[0:1]

    for l in range(DEPTH):
        h = h + hybrid_mixer(rmsnorm(h, norm_mix_g[l]), w_in[l], lb_all[l], hg_norm_g[l],
                             ret_norm_g[l], lru_conv_w[l], lru_conv_b[l], lru_gate_a_w[l],
                             lru_gate_a_b[l], lru_gate_i_w[l], lru_gate_i_b[l], lru_lambda[l],
                             w_out[l], cos, sin).astype(h.dtype)
        h = h + conv_glu_ffn(rmsnorm(h, norm_ffn_g[l]), ffn_w_up[l], ffn_conv_w[l],
                             ffn_conv_b[l], ffn_w_down[l]).astype(h.dtype)

    return rmsnorm(h, final_norm_g)[:, N_META:]


N_MIXERS = 2
N_ATTN_LAYERS = (DEPTH + 1) // 2
N_GMLP_LAYERS = DEPTH // 2
DIFF_HEADS = 8
DIFF_HEAD_DIM = D_MODEL // DIFF_HEADS // 2
DIFF_V_DIM = 2 * DIFF_HEAD_DIM
DIFF_QK_WIDTH = DIFF_HEADS * 2 * DIFF_HEAD_DIM
DIFF_V_WIDTH = DIFF_HEADS * DIFF_V_DIM
Q_BLOCK = 128
GMLP_HALF = 2 * D_MODEL
GMLP_GROUPS = 8
GMLP_CHUNK = 128
RMS_EPS = 1e-6
LN_EPS = 1e-5


def _rmsnorm(x, g):
    xf = x.astype(jnp.float32)
    y = xf * lax.rsqrt(jnp.mean(xf * xf, axis=-1, keepdims=True) + RMS_EPS)
    return (y * g.astype(jnp.float32)).astype(x.dtype)

def _layernorm(x, g, b):
    xf = x.astype(jnp.float32)
    mu = jnp.mean(xf, axis=-1, keepdims=True)
    xc = xf - mu
    var = jnp.mean(xc * xc, axis=-1, keepdims=True)
    y = xc * lax.rsqrt(var + LN_EPS) * g.astype(jnp.float32) + b.astype(jnp.float32)
    return y.astype(x.dtype)

def _swiglu_ffn(x, w_gate_up, w_down):
    g, u = jnp.split(x @ w_gate_up, 2, axis=-1)
    return (jax.nn.silu(g) * u) @ w_down

def _lambda_init(layer_idx):
    return 0.8 - 0.6 * math.exp(-0.3 * layer_idx)

def _diff_attention(h, w_in, w_out, q_norm, k_norm, lq1, lk1, lq2, lk2, subln, lam_init):
    B, S, _ = h.shape
    H, d, dv = DIFF_HEADS, DIFF_HEAD_DIM, DIFF_V_DIM
    q, k, v = jnp.split(h @ w_in, [DIFF_QK_WIDTH, 2 * DIFF_QK_WIDTH], axis=-1)
    q = _rmsnorm(q.reshape(B, S, H, 2, d), q_norm) * (d ** -0.5)
    k = _rmsnorm(k.reshape(B, S, H, 2, d), k_norm)
    v = v.reshape(B, S, H, dv)
    lam = (jnp.exp(jnp.sum(lq1.astype(jnp.float32) * lk1.astype(jnp.float32)))
           - jnp.exp(jnp.sum(lq2.astype(jnp.float32) * lk2.astype(jnp.float32)))
           + lam_init)
    outs = []
    for i in range(S // Q_BLOCK):
        L = (i + 1) * Q_BLOCK
        q_blk = q[:, i * Q_BLOCK:L]
        s = jnp.einsum('bqhcd,bkhcd->bhcqk', q_blk, k[:, :L]).astype(jnp.float32)
        qpos = i * Q_BLOCK + jnp.arange(Q_BLOCK)
        kpos = jnp.arange(L)
        mask = kpos[None, :] <= qpos[:, None]
        p = jax.nn.softmax(jnp.where(mask, s, -jnp.inf), axis=-1)
        a = (p[:, :, 0] - lam * p[:, :, 1]).astype(v.dtype)
        outs.append(jnp.einsum('bhqk,bkhe->bqhe', a, v[:, :L]))
    o = jnp.concatenate(outs, axis=1)
    o = _rmsnorm(o, subln) * (1.0 - lam_init)
    return o.reshape(B, S, DIFF_V_WIDTH) @ w_out

def _chunked_sgu(h, w_in, b_in, ln_g, ln_b, w_s, b_s, w_out, b_out):
    B, S, _ = h.shape
    z = jax.nn.gelu(h @ w_in + b_in, approximate=False)
    u, v = jnp.split(z, 2, axis=-1)
    v = _layernorm(v, ln_g, ln_b)
    nc = S // GMLP_CHUNK
    gc = GMLP_HALF // GMLP_GROUPS
    v = v.reshape(B, nc, GMLP_CHUNK, GMLP_GROUPS, gc)
    causal = jnp.tril(jnp.ones((GMLP_CHUNK, GMLP_CHUNK), dtype=bool))
    w = jnp.where(causal, w_s, 0.0)
    s = jnp.einsum('gts,bnsgc->bntgc', w, v) + jnp.transpose(b_s)[None, None, :, :, None]
    gated = u * s.reshape(B, S, GMLP_HALF)
    return gated @ w_out + b_out

def second_inputs(seed: int = 0) -> dict:
    key = jax.random.key(seed)
    ks = jax.random.split(key, 32)
    f32 = jnp.float32
    nrm = lambda k, shape, scale: jax.random.normal(k, shape, f32) * scale
    gain = lambda k, shape: 1.0 + 0.02 * jax.random.normal(k, shape, f32)
    NA, NG = N_ATTN_LAYERS, N_GMLP_LAYERS
    return {
        "x": jax.random.normal(ks[0], (BATCH, SEQ, D_MODEL), f32),
        "ffn1_norm": gain(ks[1], (DEPTH, D_MODEL)),
        "ffn1_w_gate_up": nrm(ks[2], (DEPTH, D_MODEL, 2 * D_FF), D_MODEL ** -0.5),
        "ffn1_w_down": nrm(ks[3], (DEPTH, D_FF, D_MODEL), D_FF ** -0.5),
        "mix_norm": gain(ks[4], (DEPTH, D_MODEL)),
        "ffn2_norm": gain(ks[5], (DEPTH, D_MODEL)),
        "ffn2_w_gate_up": nrm(ks[6], (DEPTH, D_MODEL, 2 * D_FF), D_MODEL ** -0.5),
        "ffn2_w_down": nrm(ks[7], (DEPTH, D_FF, D_MODEL), D_FF ** -0.5),
        "attn_w_in": nrm(ks[8], (NA, D_MODEL, 2 * DIFF_QK_WIDTH + DIFF_V_WIDTH), D_MODEL ** -0.5),
        "attn_w_out": nrm(ks[9], (NA, DIFF_V_WIDTH, D_MODEL), DIFF_V_WIDTH ** -0.5),
        "attn_q_norm": gain(ks[10], (NA, DIFF_HEAD_DIM)),
        "attn_k_norm": gain(ks[11], (NA, DIFF_HEAD_DIM)),
        "attn_lambda_q1": nrm(ks[12], (NA, DIFF_HEAD_DIM), 0.1),
        "attn_lambda_k1": nrm(ks[13], (NA, DIFF_HEAD_DIM), 0.1),
        "attn_lambda_q2": nrm(ks[14], (NA, DIFF_HEAD_DIM), 0.1),
        "attn_lambda_k2": nrm(ks[15], (NA, DIFF_HEAD_DIM), 0.1),
        "attn_subln": gain(ks[16], (NA, DIFF_V_DIM)),
        "gmlp_w_in": nrm(ks[17], (NG, D_MODEL, 2 * GMLP_HALF), D_MODEL ** -0.5),
        "gmlp_b_in": nrm(ks[18], (NG, 2 * GMLP_HALF), 0.02),
        "gmlp_ln_g": gain(ks[19], (NG, GMLP_HALF)),
        "gmlp_ln_b": nrm(ks[20], (NG, GMLP_HALF), 0.02),
        "gmlp_w_s": nrm(ks[21], (NG, GMLP_GROUPS, GMLP_CHUNK, GMLP_CHUNK), 0.5 * GMLP_CHUNK ** -0.5),
        "gmlp_b_s": gain(ks[22], (NG, GMLP_GROUPS, GMLP_CHUNK)),
        "gmlp_w_out": nrm(ks[23], (NG, GMLP_HALF, D_MODEL), GMLP_HALF ** -0.5),
        "gmlp_b_out": nrm(ks[24], (NG, D_MODEL), 0.02),
    }

def second_block(x, ffn1_norm, ffn1_w_gate_up, ffn1_w_down, mix_norm, ffn2_norm, ffn2_w_gate_up,
              ffn2_w_down, attn_w_in, attn_w_out, attn_q_norm, attn_k_norm, attn_lambda_q1,
              attn_lambda_k1, attn_lambda_q2, attn_lambda_k2, attn_subln, gmlp_w_in, gmlp_b_in,
              gmlp_ln_g, gmlp_ln_b, gmlp_w_s, gmlp_b_s, gmlp_w_out, gmlp_b_out):
    for i in range(DEPTH):
        x = x + 0.5 * _swiglu_ffn(_rmsnorm(x, ffn1_norm[i]), ffn1_w_gate_up[i], ffn1_w_down[i])
        h = _rmsnorm(x, mix_norm[i])
        j = i // N_MIXERS
        if i % N_MIXERS == 0:
            x = x + _diff_attention(h, attn_w_in[j], attn_w_out[j], attn_q_norm[j], attn_k_norm[j],
                                    attn_lambda_q1[j], attn_lambda_k1[j], attn_lambda_q2[j],
                                    attn_lambda_k2[j], attn_subln[j], _lambda_init(i))
        else:
            x = x + _chunked_sgu(h, gmlp_w_in[j], gmlp_b_in[j], gmlp_ln_g[j], gmlp_ln_b[j],
                                 gmlp_w_s[j], gmlp_b_s[j], gmlp_w_out[j], gmlp_b_out[j])
        x = x + 0.5 * _swiglu_ffn(_rmsnorm(x, ffn2_norm[i]), ffn2_w_gate_up[i], ffn2_w_down[i])
    return x


_first_inputs = second_inputs


def second_inputs(seed=0):
    import zlib

    import numpy as np

    out = dict(_first_inputs(seed))
    spreads = {}
    factors = {'ffn1_norm': 4.045,
     'ffn2_norm': 6.298,
     'attn_q_norm': 3.806,
     'attn_k_norm': 4.125,
     'attn_lambda_q2': 8.0,
     'attn_subln': 13.327,
     'gmlp_b_in': 5.564,
     'gmlp_ln_g': 64.0,
     'gmlp_ln_b': 64.0,
     'gmlp_b_s': 52.304,
     'gmlp_b_out': 34.592}
    for name, (base, spread) in spreads.items():
        noise = np.random.default_rng([zlib.crc32(name.encode()), seed]).standard_normal(out[name].shape)
        drawn = base * np.exp(spread * noise) if base else spread * noise
        out[name] = __import__('jax').numpy.asarray(drawn.astype(out[name].dtype))
    for name, factor in factors.items():
        out[name] = (out[name] * factor).astype(out[name].dtype)
    return out


_narrow_inputs = second_inputs


def second_inputs(seed=0):

    out = dict(_narrow_inputs(seed))
    wider = {'gmlp_ln_g': 8.78, 'gmlp_ln_b': 8.38, 'gmlp_b_s': 3.73, 'gmlp_b_out': 3.74}
    for name, times in wider.items():
        mean = out[name].mean()
        out[name] = (mean + times * (out[name] - mean)).astype(out[name].dtype)
    return out


def setup_inputs(seed=0):
    out = dict(first_inputs(seed))
    for name, value in second_inputs(seed + 1).items():
        if name != "x":
            out[name + "_2"] = value
    return out


def reference(
    x, meta_tokens, norm_mix_g, w_in, hg_lb_logits, hg_norm_g, ret_norm_g, lru_conv_w,
    lru_conv_b, lru_gate_a_w, lru_gate_a_b, lru_gate_i_w, lru_gate_i_b, lru_lambda, w_out,
    norm_ffn_g, ffn_w_up, ffn_conv_w, ffn_conv_b, ffn_w_down, final_norm_g, ffn1_norm_2,
    ffn1_w_gate_up_2, ffn1_w_down_2, mix_norm_2, ffn2_norm_2, ffn2_w_gate_up_2, ffn2_w_down_2,
    attn_w_in_2, attn_w_out_2, attn_q_norm_2, attn_k_norm_2, attn_lambda_q1_2, attn_lambda_k1_2,
    attn_lambda_q2_2, attn_lambda_k2_2, attn_subln_2, gmlp_w_in_2, gmlp_b_in_2, gmlp_ln_g_2,
    gmlp_ln_b_2, gmlp_w_s_2, gmlp_b_s_2, gmlp_w_out_2, gmlp_b_out_2,
):
    x = first_block(
        x, meta_tokens, norm_mix_g, w_in, hg_lb_logits, hg_norm_g, ret_norm_g, lru_conv_w,
        lru_conv_b, lru_gate_a_w, lru_gate_a_b, lru_gate_i_w, lru_gate_i_b, lru_lambda, w_out,
        norm_ffn_g, ffn_w_up, ffn_conv_w, ffn_conv_b, ffn_w_down, final_norm_g,
    )
    return second_block(
        x, ffn1_norm_2, ffn1_w_gate_up_2, ffn1_w_down_2, mix_norm_2, ffn2_norm_2,
        ffn2_w_gate_up_2, ffn2_w_down_2, attn_w_in_2, attn_w_out_2, attn_q_norm_2,
        attn_k_norm_2, attn_lambda_q1_2, attn_lambda_k1_2, attn_lambda_q2_2, attn_lambda_k2_2,
        attn_subln_2, gmlp_w_in_2, gmlp_b_in_2, gmlp_ln_g_2, gmlp_ln_b_2, gmlp_w_s_2,
        gmlp_b_s_2, gmlp_w_out_2, gmlp_b_out_2,
    )


_drawn_inputs = setup_inputs


def setup_inputs(seed=0):
    import zlib

    import numpy as np

    out = dict(_drawn_inputs(seed))
    spreads = {}
    factors = {'lru_gate_a_b': 6.231, 'lru_gate_i_b': 4.59}
    for name, (base, spread) in spreads.items():
        noise = np.random.default_rng([zlib.crc32(name.encode()), seed]).standard_normal(out[name].shape)
        drawn = base * np.exp(spread * noise) if base else spread * noise
        out[name] = __import__('jax').numpy.asarray(drawn.astype(out[name].dtype))
    for name, factor in factors.items():
        out[name] = (out[name] * factor).astype(out[name].dtype)
    return out
```

```python
from contextlib import ExitStack

import numpy as np
import concourse.bass as bass
from concourse import mybir

F32 = mybir.dt.float32
F32R = mybir.dt.float32r
ALU = mybir.AluOpType
ACT = mybir.ActivationFunctionType
AX = mybir.AxisListType
ds = bass.ds

P = 128
D = 1024
KD = D // P
META, SEQ = 16, 512
T1 = META + SEQ
T2 = SEQ
DFF = 2816
NF = DFF // P
HF = NF // 2
EPS, LN_EPS = 1e-6, 1e-5
TINY = 1e-30
ROOT_STEPS = 8
ROOT_A = 0.375 ** 0.2
ROOT_P, ROOT_Q = -1.25 / ROOT_A ** 3, 1.875 / ROOT_A
ROOT_BITS = 1594938968
HH, RH, RDK, RDV = 4, 4, 32, 64
AH, AD = 8, 64
LAM_INIT = 0.8 - 0.6
GH = 2 * D
NG = GH // P
F_MIN = 1e-19
MIX_TILES = 26
CHUNKS = [(0, META)] + [(META + P * j, P) for j in range(SEQ // P)]
LEVELS = [[8, 4, 2, 1], [64, 32, 16, 8, 4, 2, 1]]
MIX_COLS = [(512, 4), (0, 4), (1024, 4), (2048, 4), (2816, 2), (1536, 4), (2560, 2), (3072, 2)]
TILE_HF, TILE_HQ, TILE_HI, TILE_RQ, TILE_RK, TILE_RV, TILE_LX, TILE_HG, TILE_RG, TILE_LY = \
    0, 4, 8, 12, 13, 14, 16, 18, 22, 24
TAPS = 4


def param_rows():
    rows = []
    for l in range(2):
        rows += [("norm_mix_g", l, k) for k in range(KD)] + [("norm_ffn_g", l, k) for k in range(KD)]
        rows += [("hg_lb_logits", l, k) for k in range(HH)] + [("hg_norm_g", l, 0)]
        rows += [("lru_conv_w", l, k) for k in range(2 * TAPS)] + [("lru_conv_b", l, k) for k in range(2)]
        rows += [("lru_gate_a_b", l, k) for k in range(2)] + [("lru_gate_i_b", l, k) for k in range(2)]
        rows += [("lru_lambda", l, k) for k in range(2)]
        rows += [("ffn_conv_w", l, k) for k in range(3 * 2 * NF)] + [("ffn_conv_b", l, k) for k in range(2 * NF)]
    rows += [("final_norm_g", None, k) for k in range(KD)]
    for l in range(2):
        for name in ("ffn1_norm_2", "mix_norm_2", "ffn2_norm_2"):
            rows += [(name, l, k) for k in range(KD)]
    rows += [("gmlp_b_in_2", 0, k) for k in range(2 * NG)] + [("gmlp_ln_g_2", 0, k) for k in range(NG)]
    rows += [("gmlp_ln_b_2", 0, k) for k in range(NG)] + [("gmlp_b_out_2", 0, k) for k in range(KD)]
    rows += [("attn_subln_2", 0, 0)]
    rows += [("ret_norm_g", 0, 0), ("ret_norm_g", 1, 0), ("attn_q_norm_2", 0, 0), ("attn_k_norm_2", 0, 0)]
    return rows


ROWS = param_rows()
HALF_ROWS = 4
COL = {key: n for n, key in enumerate(ROWS)}
NROW_TILES = -(-len(ROWS) // P)

SQUARES = ["identity", "mean1024", "mean128", "mean64", "rotate", "causal", "future", "one"]


def constants():
    f = np.float32
    sq = {}
    sq["identity"] = np.eye(P)
    sq["one"] = np.ones((P, P))
    sq["mean1024"] = np.full((P, P), 1 / D)
    sq["mean128"] = np.full((P, P), 1 / P)
    sq["mean64"] = np.kron(np.eye(2), np.full((64, 64), 1 / 64))
    half = RDK // 2
    rot = np.zeros((P, P))
    for h in range(RH):
        for d in range(half):
            rot[RDK * h + half + d, RDK * h + d] = -1
            rot[RDK * h + d, RDK * h + half + d] = 1
    sq["rotate"] = rot
    s, t = np.arange(P)[:, None], np.arange(P)[None, :]
    sq["causal"] = (s <= t) * 1.0
    sq["future"] = np.where(t > s, -1e30, 0.0)
    squares = np.concatenate([sq[n] for n in SQUARES], 1).astype(f)
    masks = []
    for (_, n), levels in zip((CHUNKS[0], CHUNKS[1]), (LEVELS[0], LEVELS[1][1:])):
        parts = [np.eye(P)[:, :n]]
        for r in levels:
            q = np.arange(n).reshape(-1, 2, r)[:, 1, :].reshape(-1)
            first = np.arange(P)[:, None]
            parts.append(((first // (2 * r) == q // (2 * r)) & (first % (2 * r) < r)) * 1.0)
        masks.append(np.concatenate(parts, 1))
    level_masks = np.concatenate(masks, 1).astype(f)
    theta = (10000.0 ** (-np.linspace(0.0, 1.0, half, dtype=f))).astype(f)
    angle = (np.arange(T1, dtype=f)[None, :] * theta[:, None]).astype(f).astype(np.float64)
    lg = np.log1p(-np.exp2(-5.0 - np.arange(RH)))
    tabs = []
    for sign, scale in ((1, 1.0), (-1, RDK ** -0.5)):
        for fn in (np.cos, np.sin):
            a = np.concatenate([fn(angle), fn(angle)], 0)
            tabs.append(np.concatenate([a * np.exp(sign * lg[h] * np.arange(T1))[None, :] * scale
                                        for h in range(RH)], 0))
    return {"squares": squares, "level_masks": level_masks,
            "rotary": np.concatenate(tabs, 1).astype(f)}


LM0 = CHUNKS[0][1] + 8 * len(LEVELS[0])
LM1 = P + 64 * (len(LEVELS[1]) - 1)


MIX_ORDER = [("prep", 0), ("slab", 12), ("rest", 0), ("slab", 13), ("heads", 0),
             ("prep", 1), ("slab", 14), ("rest", 1), ("slab", 15), ("slab", 16), ("heads", 1),
             ("prep", 2), ("slab", 17), ("rest", 2), ("slab", 18), ("slab", 19), ("heads", 2),
             ("prep", 3), ("slab", 20), ("rest", 3), ("slab", 21), ("slab", 22), ("heads", 3),
             ("prep", 4), ("slab", 23), ("rest", 4), ("slab", 24), ("slab", 25), ("heads", 4)]
LRU_AT = {(0, 3): (0, 0), (1, 1): (1, 0), (1, 3): (0, 1), (2, 2): (1, 1)}
LAG = 4
SMALL_AT = (3, 16, 38)


class Stage:

    def __init__(self, name, slabs, kc, source, base):
        self.name, self.slabs, self.kc, self.source, self.base = name, slabs, kc, source, base


class Signal:

    def __init__(self, sem, events):
        self.sem = sem
        self.place = {e: n + 1 for n, e in enumerate(events)}

    def at(self, *event):
        return self.place[event]


def repeat(eng, start, stop, body):
    if stop - start == 1:
        body(start)
    elif stop > start:
        with eng.Fori(start, stop) as i:
            body(i)


def build(nc, a, out, upto=99):
    ctx = ExitStack()
    with ctx:
        def sb(name, cols, dt=F32):
            return ctx.enter_context(nc.sbuf_tensor(name, [P, cols], dt))

        def sem(name):
            return ctx.enter_context(nc.semaphore(name))

        h = sb("h", KD * T1)
        xhigh = sb("xhigh", KD * T1, F32R)
        xlow = sb("xlow", KD * T1, F32R)
        KC = HF
        raw = sb("raw", 2 * KC * P)
        whigh = sb("whigh", 2 * KC * P, F32R)
        wlow = sb("wlow", 2 * KC * P, F32R)
        fresh = sb("fresh", 2 * T1)
        sqr = sb("sqr", 2 * T1)
        acc = sb("acc", T1)
        rstd = sb("rstd", T1)
        par = sb("par", NROW_TILES * P)
        small = sb("small", 64)
        rcol = sb("rcol", 24)
        rcol2 = sb("rcol2", 24)
        squares = sb("squares_sb", len(SQUARES) * P)
        left = (nc.sbuf_bytes_remaining // 4) // 64 * 64 - 64
        a0 = -(-nc.sbuf_base // 64) * 64
        sb("arena", left)

        def square(name, rows=P, cols=P):
            k = SQUARES.index(name) * P
            return squares[0:rows, k:k + cols]

        def blocks(T):
            if T == T1:
                return [(0, 0, META)] + [(t, t, P) for t, _ in CHUNKS[1:]]
            return [(t, t, P) for t in range(0, T, P)]

        def by_block(bank, slot, T):
            at0 = slot * 1024 + (496 if T == T1 else 0)
            return bank[:, at0:at0 + T]

        class Region:

            def __init__(self, tag, start=0):
                self.tag, self.at = tag, start

            def sb(self, name, cols, dt=F32):
                t = nc.alloc_sbuf_tensor_at(f"{self.tag}_{name}", [P, cols], dt, offset=a0 + self.at)
                self.at += -(-cols * 4 // 32) * 32
                assert self.at <= left * 4, (self.tag, name, self.at, left * 4)
                return t

        tables_at = left * 4 // 32 * 32 - (4 * T1 + LM0 + LM1 + 8 * P) * 4 // 32 * 32 - 128
        rt = Region("tab", tables_at)
        rotary = rt.sb("rotary", 4 * T1)
        level_masks = rt.sb("level_masks", LM0 + LM1)
        gatew = rt.sb("gatew", 8 * P)

        rg = Region("load")
        rowt = rg.sb("rowt", NROW_TILES * P)
        xin = rg.sb("xin", 5 * D)
        lamv = rg.sb("lamv", 4 * AD)

        rg = Region("mix")
        hg_gate = rg.sb("hg_gate", HH * T1)
        q = rg.sb("q", HH * T1)
        v = rg.sb("v", HH * T1)
        ret_gate = rg.sb("ret_gate", 2 * T1)
        lru_gate = rg.sb("lru_gate", 2 * T1)
        rq = rg.sb("rq", T1)
        rk = rg.sb("rk", T1)
        rv = rg.sb("rv", 2 * T1)
        XP = T1 + TAPS - 1
        lx = rg.sb("lx", 2 * XP)
        shared = rg.at
        logf = rg.sb("logf", HH * T1)
        kk = rg.sb("kk", HH * T1)
        lev = rg.sb("lev", 7 * 512)
        bcum = rg.sb("bcum", 512)
        vtok = rg.sb("vtok", 512)
        ktok = rg.sb("ktok", 512)
        kdec = rg.sb("kdec", 512)
        qdec = rg.sb("qdec", 512)
        p64 = rg.sb("p64", 256)
        state = rg.sb("state", 512)
        fend = rg.sb("fend", 8)
        assert rg.at <= tables_at
        xlev, elev, psc = fresh, sqr, (acc, rstd)
        rg = Region("mix2", shared)
        cv = rg.sb("cv", 2 * T1)
        lr = rg.sb("lr", 2 * T1)
        rp = rg.sb("rp", 2 * T1)
        ro = rg.sb("ro", 2 * T1)
        rvtok = rg.sb("rvtok", 5 * 256)
        rtmp = rg.sb("rtmp", T1)
        li = rg.sb("li", 2 * T1)
        la = rg.sb("la", 2 * T1)
        lt = rg.sb("lt", 2 * T1)
        lh = rg.sb("lh", 2 * T1)
        assert rg.at <= tables_at

        rg = Region("ffn")
        hidh = rg.sb("hidh", HF * T1, F32R)
        hidl = rg.sb("hidl", HF * T1, F32R)
        zg = rg.sb("zg", T1)
        zu = rg.sb("zu", T1)
        sg = rg.sb("sg", T1)
        pr = rg.sb("pr", T1)
        assert rg.at <= tables_at

        rg = Region("att")
        qkv = rg.sb("qkv", 24 * T2)
        ex = rg.sb("ex", 2 * 2 * T2)
        aa = rg.sb("aa", 2 * T2)
        at = rg.sb("at", 2 * T2)
        avt = rg.sb("avt", 2 * T2)
        oa = rg.sb("oa", 2 * T2)
        stat = rg.sb("stat", 16)

        rg = Region("gm")
        vv = rg.sb("vv", NG * T2)
        uu = rg.sb("uu", NG * T2)
        g2h = rg.sb("g2h", KD * T2, F32R)
        g2l = rg.sb("g2l", KD * T2, F32R)
        bs = rg.sb("bs", 8 * P)
        wt = rg.sb("wt", 8 * P)
        wraw = uu
        vtm = sqr

        rg = Region("store")
        otok = rg.sb("otok", 4 * D)

        big = ctx.enter_context(nc.psum_tensor("big", [P, 2048], F32))
        misc = ctx.enter_context(nc.psum_tensor("misc", [P, 2048], F32))
        BANK = 512

        stages = []

        def stage(name, slabs, kc, source):
            base = stages[-1].base + stages[-1].slabs if stages else 0
            stages.append(Stage(name, slabs, kc, source, base))
            return stages[-1]

        def columns(w, col0, k0=0, kc=KD):
            wv = w.rearrange("(k p) c -> p k c", p=P)
            return lambda i: wv[:, k0:k0 + kc, ds(i * P + col0, P)]

        def ffn_stages(tag, w_up, w_down):
            made = []
            for half in range(2):
                gate = columns(w_up, half * HF * P)
                val = columns(w_up, DFF + half * HF * P)
                made.append(stage(f"{tag}u{half}", 2 * HF, KD, [lambda i, f=gate: f(i), lambda i, f=val: f(i)]))
                down = columns(w_down, 0, half * HF, HF)
                made.append(stage(f"{tag}d{half}", KD, HF,
                                  [lambda i, f=down: f(2 * i), lambda i, f=down: f(2 * i + 1)]))
            return made

        def plain(name, w, col0, count, kc=KD):
            f = columns(w, col0, 0, kc)
            return stage(name, count, kc, [lambda i: f(2 * i), lambda i: f(2 * i + 1)])

        plan = []
        for l in range(2):
            first = None
            for n, (c0, cnt) in enumerate(MIX_COLS):
                s = plain(f"m{l}in{n}", a["w_in"][l], c0, cnt)
                first = first or s
            plan.append(("mix", l, first, plain(f"m{l}out", a["w_out"][l], 0, KD)))
            plan.append(("cffn", l, ffn_stages(f"c{l}", a["ffn_w_up"][l], a["ffn_w_down"][l])))
        plan.append(("final", 0))
        for l in range(2):
            plan.append(("ffn", 2 * l, ffn_stages(f"g{l}", a["ffn1_w_gate_up_2"][l], a["ffn1_w_down_2"][l])))
            if l == 0:
                plan.append(("attn", 0, plain("ain", a["attn_w_in_2"][0], 0, 24),
                             plain("aout", a["attn_w_out_2"][0], 0, KD)))
            else:
                sv = plain("gv", a["gmlp_w_in_2"][0], GH, NG)
                su = plain("gu", a["gmlp_w_in_2"][0], 0, NG)
                lo = columns(a["gmlp_w_out_2"][0], 0, 0, KD)
                hi = columns(a["gmlp_w_out_2"][0], 0, KD, KD)
                so = stage("gout", 2 * KD, KD, [lambda i: lo(i), lambda i: hi(i)])
                plan.append(("gmlp", 0, sv, su, so))
            plan.append(("ffn", 2 * l + 1, ffn_stages(f"f{l}", a["ffn2_w_gate_up_2"][l], a["ffn2_w_down_2"][l])))
        plan = plan[:upto]
        used = [x for ph in plan for x in ph[2:] for x in (x if isinstance(x, list) else [x])]
        for ph in plan:
            if ph[0] == "mix":
                used += [s for s in stages if s.name.startswith(f"m{ph[1]}in")]
        stages = [s for s in stages if s in used]
        n_slabs = stages[-1].base + stages[-1].slabs
        kc_of = [s.kc for s in stages for _ in range(s.slabs)]

        norm_of, tile_of, fill_of = {}, {}, {}
        norms, tiles, fills, norm_T = 0, 0, 0, []
        for n, ph in enumerate(plan):
            T = T1 if n < 5 else T2
            norm_of[n], tile_of[n] = norms, tiles
            norms += 1
            norm_T.append(T)
            fill_of[n] = fills
            if ph[0] == "final":
                continue
            fills += KD
            if ph[0] == "mix":
                tiles += MIX_TILES + KD
                fills += KD
            elif ph[0] == "attn":
                tiles += 24 + KD
                fills += KD
            elif ph[0] == "gmlp":
                tiles += 2 * NG + KD
                fills += NG
            else:
                tiles += 2 * (2 * HF + KD)
        FFN_AT = {}
        for n, ph in enumerate(plan):
            if ph[0] in ("cffn", "ffn"):
                FFN_AT[n] = NF * len(FFN_AT)

        x_in = [sem(f"x_in{n}") for n in range(5)]
        par_in, tab_in, gatew_in, lam_in, ws_in = [sem(n) for n in ("par_in", "tab_in", "gatew_in", "lam_in", "ws_in")]
        gate_zero, squares_in, par_in_soft = sem("gate_zero"), sem("squares_in"), sem("par_in_soft")
        x_turned, par_turned = sem("x_turned"), sem("par_turned")
        par_ready, small_step = sem("par_ready"), sem("small_step")
        small_act = sem("small_act")
        h_loaded = sem("h_loaded")
        raw_in = [sem(f"raw_in{n}") for n in range(2)]
        high_rounded = sem("high_rounded")
        slab_split = sem("slab_split")
        slab_done = sem("slab_done")
        tile_out = [sem(f"tile_out{n}") for n in range(2)]
        squared, summed = sem("squared"), sem("summed")
        ms_done, rstd_ready = sem("ms_done"), sem("rstd_ready")
        rstd_spread, rstd_wide = sem("rstd_spread"), sem("rstd_wide")
        fresh_ready, xhigh_ready, x_ready = sem("fresh_ready"), sem("xhigh_ready"), sem("x_ready")
        final_done = sem("final_done")
        z_ready = sem("z_ready")
        conv_step, silu_ready = sem("conv_step"), sem("silu_ready")
        prod_ready, hidh_ready, hid_ready = sem("prod_ready"), sem("hidh_ready"), sem("hid_ready")
        store_turned, store_copied, stored = sem("store_turned"), sem("store_copied"), sem("stored")

        L2 = range(2)
        CH = range(len(CHUNKS))
        steps = [(l, c, j) for l in L2 for c in CH for j in range(2 + len(LEVELS[c > 0]))]
        fk_ready = Signal(sem("fk_ready"), [(l, i) for l in L2 for i in range(HH)])
        logf_ready = Signal(sem("logf_ready"), [(l,) for l in L2])
        decay_ready = Signal(sem("decay_ready"), [x for x in steps if x[2]])
        exp_ready = Signal(sem("exp_ready"), steps)
        lev_ready = Signal(sem("lev_ready"), steps)
        scanned = Signal(sem("scanned"), [(l, c) for l in L2 for c in CH])
        turned = Signal(sem("turned"), [(l, c, x) for l in L2 for c in CH for x in "vk"])
        tok_ready = Signal(sem("tok_ready"), [(l, c, x) for l in L2 for c in CH for x in "vk"])
        scored = Signal(sem("scored"), [(l, c, i) for l in L2 for c in CH for i in range(HH)])
        masked = Signal(sem("masked"), [(l, c, i) for l in L2 for c in CH for i in range(HH)])
        headout = Signal(sem("headout"), [(l, c, i) for l in L2 for c in CH for i in range(HH)])
        scored64 = Signal(sem("scored64"), [(l, c) for l in L2 for c in CH if c])
        p64_ready = Signal(sem("p64_ready"), [(l, c) for l in L2 for c in CH if c])
        upd_done = Signal(sem("upd_done"), [(l, c) for l in L2 for c in CH[:-1]])
        state_ready = Signal(sem("state_ready"), [(l, c) for l in L2 for c in CH[:-1]])
        o_ready = Signal(sem("o_ready"), [(l, c) for l in L2 for c in CH])
        gates_ready = Signal(sem("gates_ready"), [(l, x) for l in L2 for x in ("hg", "ret", "lru")])
        osq_ready = Signal(sem("osq_ready"), [(l,) for l in L2])
        oms_done = Signal(sem("oms_done"), [(l,) for l in L2])
        orstd = Signal(sem("orstd"), [(l,) for l in L2])
        ospread = Signal(sem("ospread"), [(l, i) for l in L2 for i in range(HH)])
        oscaled = Signal(sem("oscaled"), [(l, i) for l in L2 for i in range(HH)])
        rotated = Signal(sem("rotated"), [(l, x) for l in L2 for x in "qk"])
        rope_step = Signal(sem("rope_step"), [(l, x, n) for l in L2 for x in "qk" for n in range(3)])
        rvturned = Signal(sem("rvturned"), [(l,) for l in L2])
        rvtok_ready = Signal(sem("rvtok_ready"), [(l,) for l in L2])
        units = [(l, i, c) for l in L2 for i in range(RH) for c in CH]
        rscored = Signal(sem("rscored"), units)
        rdiag = Signal(sem("rdiag"), units)
        rrest = Signal(sem("rrest"), [u for u in units if u[2] < len(CHUNKS) - 1])
        rapplied = Signal(sem("rapplied"), units)
        pairs = [(l, p) for l in L2 for p in range(2)]
        ro_ready = Signal(sem("ro_ready"), pairs)
        rmean = Signal(sem("rmean"), pairs)
        rcentred = Signal(sem("rcentred"), pairs)
        rsq = Signal(sem("rsq"), pairs)
        rvar = Signal(sem("rvar"), [(l,) for l in L2])
        rrstd = Signal(sem("rrstd"), [(l,) for l in L2])
        rspread = Signal(sem("rspread"), pairs)
        rnormed = Signal(sem("rnormed"), pairs)
        pad_zero = Signal(sem("pad_zero"), [(l,) for l in L2])
        cv_start = Signal(sem("cv_start"), pairs)
        cv_step = Signal(sem("cv_step"), [(l, p, n) for l, p in pairs for n in range(3)])
        gated = Signal(sem("gated"), [(l, p, x) for l, p in pairs for x in "ai"])
        gsig = Signal(sem("gsig"), [(l, p, x) for l, p in pairs for x in "ai"])
        lru_exp = Signal(sem("lru_exp"), pairs)
        lru_step = Signal(sem("lru_step"), [(l, p, n) for l, part in ((l, part) for l in L2 for part in ((0, 0), (1, 0), (0, 1), (1, 1)))
                                           for p in part[:1] for n in (range(4) if part[1] == 0 else range(4, 6))])
        lru_root = Signal(sem("lru_root"), pairs)
        root_step = sem("root_step")

        qms_done, qrstd, qn_ready = sem("qms_done"), sem("qrstd"), sem("qn_ready")
        ascored, amasked, amax_ready = sem("ascored"), sem("amasked"), sem("amax_ready")
        aexp_ready, astep, a_ready = sem("aexp_ready"), sem("astep"), sem("a_ready")
        aturned, atok_ready, aapplied = sem("aturned"), sem("atok_ready"), sem("aapplied")
        ao_ready, aosq, aoms, aorstd = sem("ao_ready"), sem("aosq"), sem("aoms"), sem("aorstd")
        aospread = sem("aospread")
        ws_turned, ws_ready = sem("ws_turned"), sem("ws_ready")
        g_sum, g_stat, g_statv = sem("g_sum"), sem("g_stat"), sem("g_statv")
        g_centred, g_sq, g_scaled, g_affine = sem("g_centred"), sem("g_sq"), sem("g_scaled"), sem("g_affine")
        g_turned, g_tok, g_mixed, g_step = sem("g_turned"), sem("g_tok"), sem("g_mixed"), sem("g_step")

        def hc(k, T=T1):
            return h[:, ds(k * T1 + (T1 - T), T)]

        def c1(t, k, n=T1, off=0):
            return t[:, ds(k * T1 + off, n)]

        def c2(t, k, n=T2, off=0):
            return t[:, ds(k * T2 + off, n)]

        def pcol(name, l, k=0):
            c = COL[(name, l, k)]
            return par[:, c:c + 1]

        def pdyn(name, l, k):
            return par[:, ds(COL[(name, l, 0)] + k, 1)]

        def wide(ps, slot, T):
            at0 = slot * 1024 + (BANK - T1 // 2 if T == T1 else 0)
            return ps[:, at0:at0 + T]

        def parts(T):
            return [(0, T // 2), (T // 2, T // 2)] if T == T1 else [(0, T)]

        S_LB, S_OML, S_OMLS, S_SP, S_NSP, S_GQ, S_SUB, S_NLAM, S_TMP = 0, 8, 16, 24, 28, 32, 33, 34, 36

        def sm(c, n=1):
            return small[:, c:c + n]

        def load_slab(eng, st, s, i, n):
            if not isinstance(n, int) or n >= 2:
                eng.wait_ge(slab_split, n - 1)
            dst = raw[:, s * KC * P:s * KC * P + st.kc * P].rearrange("p (k c) -> p k c", c=P)
            eng.dma_start(dst, st.source[s](i)).then_inc(raw_in[s], 16)

        par_loads = []
        n = 0
        while n < len(ROWS):
            name, l, _ = ROWS[n]
            src = a[name] if l is None else a[name][l]
            if n >= len(ROWS) - HALF_ROWS:
                for half in range(2):
                    c0 = n // P * P + 64 * half
                    par_loads.append((rowt[n % P:n % P + 1, c0:c0 + 64], src.rearrange("(o c) -> o c", o=1)))
                n += 1
                continue
            m = n
            while m < len(ROWS) and ROWS[m][:2] == (name, l):
                m += 1
            flat = src if len(src.shape) == 1 else src.rearrange("j c -> (j c)")
            flat = flat.rearrange("(r c) -> r c", c=P)
            k = n
            while k < m:
                e = min(m, (k // P + 1) * P)
                par_loads.append((rowt[k % P:k % P + e - k, k // P * P:(k // P + 1) * P], flat[k - n:e - n, :]))
                k = e
            n = m

        block = ctx.enter_context(nc.Block())

        @block.sync
        def _(eng):
            eng.dma_start(xin[0:META, 0:D], a["meta_tokens"]).then_inc(x_in[0], 16)
            for j in range(4):
                eng.dma_start(xin[:, (j + 1) * D:(j + 2) * D], a["x"][0, P * j:P * j + P, :]).then_inc(x_in[j + 1], 16)
            for dst, src in par_loads[1::3]:
                eng.dma_start(dst, src).then_inc(par_in, 16)
            eng.dma_start(rotary[:, :], a["rotary"]).then_inc(tab_in, 16)
            eng.dma_start(level_masks[:, :], a["level_masks"]).then_inc(tab_in, 16)
            for k, name in enumerate(("attn_lambda_q1_2", "attn_lambda_k1_2", "attn_lambda_q2_2", "attn_lambda_k2_2")):
                eng.dma_start(lamv[:, k * AD:(k + 1) * AD], a[name][0].partition_broadcast(P)).then_inc(lam_in, 16)
            for st in stages:
                def pair(i, st=st):
                    for s in range(2):
                        load_slab(eng, st, s, i, st.base + 2 * i + s)
                if st.base == 0:
                    pair(0)
                    eng.wait_ge(gate_zero, 1)
                    for l in L2:
                        for g, name in enumerate(("lru_gate_a_w", "lru_gate_i_w")):
                            for half in range(2):
                                c0 = (l * 2 + g) * 2 * P
                                dst = gatew[64 * half:64 * half + 64, c0:c0 + 2 * P].rearrange(
                                    "p (c e) -> p c e", c=2)[:, :, 64 * half:64 * half + 64]
                                src = a[name][l].rearrange("(c b) d e -> b d c e", b=2)[half]
                                eng.dma_start(dst, src).then_inc(gatew_in, 16)
                    repeat(eng, 1, st.slabs // 2, pair)
                else:
                    repeat(eng, 0, st.slabs // 2, pair)
            for tb in range(4):
                eng.wait_ge(store_copied, 2 * tb + 2)
                eng.dma_start(out[P * tb:P * tb + P, :], otok[:, tb * D:(tb + 1) * D]).then_inc(stored, 16)
            eng.wait_ge(stored, 64)

        @block.gpsimd
        def _(eng):
            eng.memset(gatew[:, :], 0.0).then_inc(gate_zero, 1)
            for dst, src in par_loads[2::3]:
                eng.dma_start(dst, src).then_inc(par_in_soft, 16)
            for st in stages:
                if st.name == "gv":
                    eng.wait_ge(slab_done, st.base)
                    eng.dma_start(wraw[:, 0:8 * P].rearrange("p (g s) -> p g s", g=8),
                                  a["gmlp_w_s_2"][0].rearrange("g t s -> t g s")).then_inc(ws_in, 16)
                    src = a["gmlp_b_s_2"][0].rearrange("g t -> (g t)").partition_broadcast(P)
                    eng.dma_start(bs[:, :], src).then_inc(ws_in, 16)

                def pair(i, st=st):
                    for s in range(2):
                        at0, n = s * KC * P, st.kc * P
                        eng.wait_ge(high_rounded, st.base + 2 * i + s + 1)
                        eng.tensor_tensor(wlow[:, at0:at0 + n], raw[:, at0:at0 + n],
                                          whigh[:, at0:at0 + n].bitcast(F32), ALU.subtract).then_inc(slab_split, 1)
                repeat(eng, 0, st.slabs // 2, pair)

        @block.scalar
        def _(eng):
            def high_part(st, s, i):
                n = st.base + 2 * i + s
                at0, w = s * KC * P, st.kc * P
                eng.wait_ge(raw_in[s], 16 * (st.base // 2 + i + 1))
                if not isinstance(n, int) or n >= 2:
                    eng.wait_ge(slab_done, n - 1)
                eng.copy(whigh[:, at0:at0 + w], raw[:, at0:at0 + w]).then_inc(high_rounded, 1)

            def high_of(n):
                if n < n_slabs:
                    st = [s for s in stages if s.base <= n < s.base + s.slabs][0]
                    high_part(st, (n - st.base) % 2, (n - st.base) // 2)

            def slab_loop(st, body):
                last = st.slabs // 2 - 1
                body(0, lambda s: high_part(st, s, 1))
                repeat(eng, 1, last, lambda i: body(i, lambda s: high_part(st, s, i + 1)))
                body(last, lambda s: high_of(st.base + 2 * last + s + 2))

            eng.dma_start(squares[:, :], a["squares"]).then_inc(squares_in, 16)
            for dst, src in par_loads[0::3]:
                eng.dma_start(dst, src).then_inc(par_in, 16)
            def squares_of(j, k, s, T):
                if not isinstance(k, int) or k >= 2:
                    eng.wait_ge(summed, 9 * j + k)
                eng.activation(c1(sqr, s, T), hc(k, T), ACT.Square).then_inc(squared, 1)

            def split_fresh(q, dst):
                eng.wait_ge(fresh_ready, q + 1)
                n = dst.shape[-1]
                eng.copy(dst, c1(fresh, q % 2, n)).then_inc(xhigh_ready, 1)

            SMALL_EXPS = ((S_TMP, S_TMP, 8), (S_TMP + 8, S_TMP + 8, 4), (S_TMP + 12, S_TMP + 12, 2))
            for k in range(KD):
                eng.wait_ge(h_loaded, k + 1)
                squares_of(0, k, k % 2, T1)
            high_of(0)
            high_of(1)

            def residual_squares(st, n, tile0, T):
                def body(i, ahead):
                    for s in range(2):
                        ahead(s)
                        if norm_of[n] + 1 < norms:
                            eng.wait_ge(tile_out[s], tile0 // 2 + i + 1)
                            squares_of(norm_of[n] + 1, 2 * i + s, s, T)
                slab_loop(st, body)

            def residual_squares2(st, n, tile0, T):
                def one(i, s, ahead):
                    for x in range(2):
                        ahead(x)
                    if norm_of[n] + 1 < norms:
                        eng.wait_ge(tile_out[s], tile0 // 2 + i + 1)
                        squares_of(norm_of[n] + 1, 2 * i + s, s, T)

                def two(i):
                    one(i, 0, lambda x: high_part(st, x, 2 * i + 1))
                    one(i, 1, lambda x: high_part(st, x, 2 * i + 2))
                last = st.slabs // 4 - 1
                two(0)
                repeat(eng, 1, last, two)
                one(last, 0, lambda x: high_part(st, x, 2 * last + 1))
                one(last, 1, lambda x: high_of(st.base + st.slabs + x))

            def ffn(n, ph):
                T = T1 if ph[0] == "cffn" else T2
                j0 = FFN_AT[n]
                for half in range(2):
                    up, down = ph[2][2 * half:2 * half + 2]
                    tile0 = tile_of[n] + half * (2 * HF + KD)
                    first = j0 + half * HF

                    def body(i, ahead):
                        f = half * HF + i
                        ahead(0)
                        eng.wait_ge(slab_done, up.base + 2 * i + 1)
                        done = not (isinstance(i, int) and first + i == 0)
                        if ph[0] == "cffn":
                            l = ph[1]
                            if done:
                                eng.wait_ge(silu_ready, first + i)
                            eng.activation(zg[:, :], wide(big, 0, T), ACT.Identity, bias=pdyn("ffn_conv_b", l, f),
                                           scale=pdyn("ffn_conv_w", l, 2 * 2 * NF + f)).then_inc(z_ready, 1)
                            ahead(1)
                            eng.wait_ge(slab_done, up.base + 2 * i + 2)
                            if done:
                                eng.wait_ge(prod_ready, first + i)
                            eng.activation(zu[:, :], wide(big, 1, T), ACT.Identity,
                                           bias=pdyn("ffn_conv_b", l, NF + f),
                                           scale=pdyn("ffn_conv_w", l, 2 * 2 * NF + NF + f)).then_inc(z_ready, 1)
                            eng.wait_ge(tile_out[0], tile0 // 2 + i + 1)
                            eng.activation(sg[:, :], zg[:, :], ACT.Silu).then_inc(silu_ready, 1)
                        else:
                            eng.wait_ge(tile_out[1], tile0 // 2 + i)
                            eng.activation(sg[:, 0:T], wide(big, 0, T), ACT.Silu).then_inc(tile_out[0], 1)
                            ahead(1)
                    slab_loop(up, body)
                    if half == 0:
                        slab_loop(down, lambda i, ahead: (ahead(0), ahead(1)))
                    else:
                        residual_squares(down, n, tile0 + 2 * HF, T)

            def mix(n, ph):
                l, first, wout = ph[1], ph[2], ph[3]
                s0, t0, q0 = first.base, tile_of[n], fill_of[n]

                def begin(i):
                    high_of(s0 + i + 2)
                    eng.wait_ge(slab_done, s0 + i + 1)

                def leave(ins, i):
                    ins.then_inc(tile_out[i % 2], 1)

                def tile(i):
                    begin(i)
                    src = wide(big, i % 2, T1)
                    if i < TILE_HQ:
                        eng.activation(c1(logf, i), src, ACT.Sigmoid)
                        leave(eng.activation(c1(kk, i), src, ACT.Sigmoid, scale=-1.0), i)
                    elif i < TILE_HI:
                        leave(eng.activation(c1(q, i - TILE_HQ), src, ACT.Silu), i)
                    elif i in (TILE_LX, TILE_LX + 1):
                        c = i - TILE_LX
                        leave(eng.copy(lx[:, c * XP + TAPS - 1:(c + 1) * XP], src), i)
                    else:
                        for lo, t, m in ((TILE_HI, v, 4), (TILE_RQ, rq, 1), (TILE_RK, rk, 1), (TILE_RV, rv, 2),
                                         (TILE_HG, hg_gate, 4), (TILE_RG, ret_gate, 2), (TILE_LY, lru_gate, 2)):
                            if lo <= i < lo + m:
                                leave(eng.copy(c1(t, i - lo), src), i)

                def prep(c, part):
                    _, w = CHUNKS[c]
                    b = bcum[:, 0:4 * w]
                    g0 = steps.index((l, c, 0))
                    if part == 0:
                        eng.wait_ge(scanned.sem, scanned.at(l, c))
                        if c < len(CHUNKS) - 1:
                            if c >= 2:
                                eng.wait_ge(state_ready.sem, state_ready.at(l, c - 2))
                            elif l:
                                eng.wait_ge(state_ready.sem, state_ready.at(l - 1, 3))
                            eng.activation(fend[:, 4 * (c % 2):4 * (c % 2) + 4],
                                           b.rearrange("p (i t) -> p i t", i=HH)[:, :, w - 1], ACT.Exp)
                    for j in range(0, 3) if part == 0 else range(3, 2 + len(LEVELS[c > 0])):
                        g = g0 + j
                        e = elev[:, (g % 2) * T1:(g % 2) * T1 + 4 * w]
                        x = xlev[:, (g % 2) * T1:(g % 2) * T1 + 4 * w]
                        if g >= 2:
                            eng.wait_ge(lev_ready.sem, g - 1)
                        if j == 0:
                            eng.activation(e, b, ACT.Exp).then_inc(exp_ready.sem, 1)
                            continue
                        eng.wait_ge(decay_ready.sem, decay_ready.at(l, c, j))
                        if j == 1:
                            eng.activation(e, x, ACT.Exp, scale=-1.0).then_inc(exp_ready.sem, 1)
                            continue
                        r = LEVELS[c > 0][j - 2]
                        ev = e.rearrange("p (g two r) -> p g two r", two=2, r=r)
                        xv = x.rearrange("p (g two r) -> p g two r", two=2, r=r)
                        eng.activation(ev[:, :, 0, :], xv[:, :, 0, :], ACT.Exp, scale=-1.0)
                        eng.activation(ev[:, :, 1, :], xv[:, :, 1, :], ACT.Exp).then_inc(exp_ready.sem, 1)

                def heads(c):
                    tk, w = CHUNKS[c]
                    if c:
                        if c < len(CHUNKS):
                            eng.wait_ge(upd_done.sem, upd_done.at(l, c - 1))
                    elif l:
                        eng.wait_ge(headout.sem, headout.at(l - 1, len(CHUNKS) - 1, HH - 1))
                    eng.wait_ge(turned.sem, turned.at(l, c, "v"))
                    eng.copy(vtok[0:w, :], misc[0:w, 0:512]).then_inc(tok_ready.sem, 1)
                    eng.wait_ge(turned.sem, turned.at(l, c, "k"))
                    eng.copy(ktok[0:w, :], misc[0:w, BANK:BANK + 512]).then_inc(tok_ready.sem, 1)
                    if c:
                        eng.wait_ge(scored64.sem, scored64.at(l, c))
                        eng.copy(p64[0:64, :], misc[0:64, BANK:BANK + 256]).then_inc(p64_ready.sem, 1)
                    eng.wait_ge(headout.sem, headout.at(l, c, HH - 1))
                    eng.copy(q[:, :].rearrange("p (i t) -> p i t", i=HH)[:, :, tk:tk + w],
                             misc[:, 0:512].rearrange("p (i t) -> p i t", i=HH)[:, :, 0:w]).then_inc(o_ready.sem, 1)

                for k in range(KD):
                    split_fresh(q0 + k, c1(xhigh, k))
                for i in range(8):
                    tile(i)
                    if n == 0 and i < len(SMALL_EXPS):
                        src, dst, cols = SMALL_EXPS[i]
                        eng.wait_ge(small_step, SMALL_AT[i])
                        eng.activation(sm(dst, cols), sm(src, cols), ACT.Exp).then_inc(small_act, 1)
                for i in range(HH):
                    eng.wait_ge(fk_ready.sem, fk_ready.at(l, i))
                    ins = eng.activation(c1(logf, i), c1(logf, i), ACT.Ln, bias=sm(S_LB + 4 * l + i))
                ins.then_inc(logf_ready.sem, 1)
                for i in range(8, 12):
                    tile(i)
                for what, x in MIX_ORDER:
                    if what == "slab":
                        tile(x)
                    elif what == "heads":
                        heads(x)
                    else:
                        prep(x, part=what == "rest")
                eng.wait_ge(o_ready.sem, o_ready.at(l, len(CHUNKS) - 1))
                eng.activation(kk[:, :], q[:, :], ACT.Square).then_inc(osq_ready.sem, 1)
                eng.wait_ge(tile_out[1], (t0 + MIX_TILES) // 2)
                for p in range(2):
                    eng.activation(c1(cv, p), lx[:, p * XP + TAPS - 1:(p + 1) * XP], ACT.Identity,
                                   bias=pcol("lru_conv_b", l, p), scale=pcol("lru_conv_w", l, 2 * (TAPS - 1) + p)
                                   ).then_inc(cv_start.sem, 1)
                eng.activation(hg_gate[:, :], hg_gate[:, :], ACT.Silu).then_inc(gates_ready.sem, 1)
                for p in range(2):
                    for x, (name, dst) in enumerate((("lru_gate_a_b", lr), ("lru_gate_i_b", li))):
                        eng.wait_ge(gated.sem, gated.at(l, p, "ai"[x]))
                        eng.activation(c1(dst, p), wide(big, x, T1), ACT.Sigmoid, bias=pcol(name, l, p)
                                       ).then_inc(gsig.sem, 1)
                for k in range(HH):
                    split_fresh(q0 + KD + k, c1(xhigh, k))
                eng.wait_ge(rvturned.sem, rvturned.at(l))
                eng.copy(rvtok[0:META, 0:256], big[0:META, 0:256])
                eng.copy(rvtok[:, 256:1280], big[:, 256:1280]).then_inc(rvtok_ready.sem, 1)
                for p in range(2):
                    eng.wait_ge(gsig.sem, gsig.at(l, 1, "i"))
                    eng.activation(c1(la, p), c1(lr, p), ACT.Exp, scale=sm(S_NSP + 2 * l + p))
                    eng.activation(c1(lt, p), c1(lr, p), ACT.Tanh, scale=sm(S_SP + 2 * l + p)).then_inc(lru_exp.sem, 1)
                for i in range(RH):
                    for c, (tk, w) in enumerate(CHUNKS[:-1]):
                        u = units.index((l, i, c))
                        sl = u % 2
                        if (i, c) == (1, 2):
                            for p in range(2):
                                eng.wait_ge(lru_step.sem, lru_step.at(l, p, 3))
                                eng.activation(c1(lt, p), c1(lt, p), ACT.Sqrt).then_inc(lru_root.sem, 1)
                        eng.wait_ge(rdiag.sem, u + 1)
                        if u >= 2:
                            eng.wait_ge(rapplied.sem, u - 1)
                        eng.copy(rp[0:w, sl * T1 + w:sl * T1 + T1 - tk],
                                 misc[0:w, sl * 1024 + 496 + tk + w:sl * 1024 + 1024]).then_inc(rrest.sem, 1)
                for p in range(2):
                    eng.wait_ge(rapplied.sem, rapplied.at(l, 2 * p + 1, len(CHUNKS) - 1))
                    eng.copy(c1(ro, p), big[:, p * 1024 + 496:(p + 1) * 1024]).then_inc(ro_ready.sem, 1)
                for p in range(2):
                    eng.wait_ge(rcentred.sem, rcentred.at(l, p))
                    eng.activation(c1(rp, p), c1(ro, p), ACT.Square).then_inc(rsq.sem, 1)
                eng.activation(ret_gate[:, :], ret_gate[:, :], ACT.Silu).then_inc(gates_ready.sem, 1)
                eng.activation(lru_gate[:, :], lru_gate[:, :], ACT.Gelu_apprx_tanh).then_inc(gates_ready.sem, 1)
                for p in range(2):
                    split_fresh(q0 + KD + 4 + p, c1(xhigh, 4 + p))
                for p in range(2):
                    split_fresh(q0 + KD + 6 + p, c1(xhigh, 6 + p))
                residual_squares(wout, n, t0 + MIX_TILES, T1)

            def attn(n, ph):
                win, wout = ph[2], ph[3]
                s0, t0, q0 = win.base, tile_of[n], fill_of[n]

                def body(i, ahead):
                    for s in range(2):
                        ahead(s)
                        eng.wait_ge(slab_done, s0 + 2 * i + s + 1)
                        eng.copy(c2(qkv, 2 * i + s), wide(big, s, T2))
                        if not isinstance(i, int) or i:
                            eng.wait_ge(qms_done, 2 * i + s - 1)
                        eng.activation(c1(sqr, s, T2), wide(big, s, T2), ACT.Square).then_inc(tile_out[s], 1)

                def vbody(i, ahead):
                    for s in range(2):
                        ahead(s)
                        eng.wait_ge(slab_done, s0 + 16 + 2 * i + s + 1)
                        eng.copy(c2(qkv, 2 * i + s + 16), wide(big, s, T2)).then_inc(tile_out[s], 1)
                body(0, lambda s: high_part(win, s, 1))
                repeat(eng, 1, 8, lambda i: body(i, lambda s: high_part(win, s, i + 1)))
                repeat(eng, 0, 3, lambda i: vbody(i, lambda s: high_part(win, s, i + 9)))
                vbody(3, lambda s: high_of(s0 + 24 + s))

                def exps(u):
                    L = (u % 4 + 1) * P
                    sl = u % 2
                    eng.wait_ge(amax_ready, u + 1)
                    if u >= 2:
                        eng.wait_ge(a_ready, u - 1)
                    for c in range(2):
                        ins = eng.activation(ex[:, sl * 1024 + c * 512:sl * 1024 + c * 512 + L],
                                             misc[:, sl * 1024 + c * 512:sl * 1024 + c * 512 + L], ACT.Exp,
                                             bias=stat[:, 2 * sl + c:2 * sl + c + 1],
                                             accum_out=stat[:, 4 + 2 * sl + c:5 + 2 * sl + c])
                    ins.then_inc(aexp_ready, 1)

                def copy_turned(k):
                    m, b = k // 5, k % 5
                    eng.wait_ge(aturned, k + 1)
                    src = big[:, (k % 2) * 512:(k % 2) * 512 + 512]
                    if b == 0:
                        if m >= 2:
                            eng.wait_ge(aapplied, 4 * (m - 1))
                        eng.copy(c2(avt, m % 2), src).then_inc(atok_ready, 1)
                    else:
                        u = 4 * m + b - 1
                        if u >= 2:
                            eng.wait_ge(aapplied, u - 1)
                        eng.copy(c2(at, u % 2, b * P), src[:, 0:b * P]).then_inc(atok_ready, 1)

                def out_head(m):
                    eng.wait_ge(aapplied, 4 * m + 4)
                    if m >= 2:
                        eng.wait_ge(fresh_ready, q0 + KD + m - 1)
                    eng.copy(c2(oa, m % 2), big[:, 1024 + (m % 2) * 512:1536 + (m % 2) * 512]).then_inc(ao_ready, 1)
                    if m >= 2:
                        eng.wait_ge(aoms, m - 1)
                    eng.wait_ge(ao_ready, m + 1)
                    eng.activation(c1(sqr, m % 2, T2), c2(oa, m % 2), ACT.Square).then_inc(aosq, 1)

                copy_turned(0)
                exps(0)
                for u in range(32):
                    m, b = u // 4, u % 4
                    if u + 1 < 32:
                        exps(u + 1)
                    copy_turned(5 * m + b + 1)
                    if b == 0 and m:
                        out_head(m - 1)
                    if b == 3 and m:
                        split_fresh(q0 + KD + m - 1, c1(xhigh, m - 1, T2))
                    if b == 3 and m < 7:
                        copy_turned(5 * (m + 1))
                out_head(7)
                split_fresh(q0 + KD + 7, c1(xhigh, 7, T2))
                residual_squares(wout, n, t0 + 24, T2)

            def gmlp(n, ph):
                sv, su, so = ph[2:]
                t0, q0 = tile_of[n], fill_of[n]

                def gelu_tile(st, dst, tb, bias0, i, s):
                    eng.wait_ge(slab_done, st.base + 2 * i + s + 1)
                    eng.activation(c2(dst, 2 * i + s), wide(big, s, T2), ACT.Gelu,
                                   bias=pdyn("gmlp_b_in_2", 0, bias0 + 2 * i + s)).then_inc(tile_out[s], 1)

                def vbody(i, ahead):
                    for s in range(2):
                        ahead(s)
                        gelu_tile(sv, vv, t0, NG, i, s)
                slab_loop(sv, vbody)

                def square(m):
                    eng.wait_ge(g_centred, m + 1)
                    if m >= 2:
                        eng.wait_ge(g_sum, 1 + NG + 1 + m - 1)
                    eng.activation(c1(sqr, m % 2, T2), c2(vv, m), ACT.Square).then_inc(g_sq, 1)

                def affine(m):
                    eng.wait_ge(g_scaled, m + 1)
                    eng.activation(c2(vv, m), c2(vv, m), ACT.Identity, bias=pcol("gmlp_ln_b_2", 0, m),
                                   scale=pcol("gmlp_ln_g_2", 0, m)).then_inc(g_affine, 1)
                sq_m, af_m = 0, 0
                for i in range(NG // 2):
                    for s in range(2):
                        high_of(su.base + 2 * i + s + 2)
                        gelu_tile(su, uu, t0, 0, i, s)
                        if 1 <= i < 5:
                            square(sq_m)
                            square(sq_m + 1)
                            sq_m += 2
                        elif i >= 5:
                            for _ in range(3 if af_m + 3 <= NG else NG - af_m):
                                affine(af_m)
                                af_m += 1
                while af_m < NG:
                    affine(af_m)
                    af_m += 1
                for m in range(NG + 1):
                    if m < NG:
                        eng.wait_ge(g_turned, m + 1)
                        if m >= 2:
                            eng.wait_ge(g_mixed, m - 1)
                        eng.copy(c1(vtm, m % 2, T2), misc[:, (m % 2) * 1024:(m % 2) * 1024 + 512]).then_inc(g_tok, 1)
                    if m >= 1:
                        k = m - 1
                        split_fresh(q0 + KD + k, c1(xhigh, k, T2) if k < KD else c2(g2h, k - KD))
                residual_squares2(so, n, t0 + 2 * NG, T2)

            for n, ph in enumerate(plan):
                if ph[0] == "mix":
                    mix(n, ph)
                    continue
                if ph[0] == "final":
                    for k in range(KD if norm_of[n] + 1 < norms else 0):
                        eng.wait_ge(final_done, k + 1)
                        squares_of(norm_of[n] + 1, k, k % 2, T2)
                    continue
                T = norm_T[norm_of[n]]
                for k in range(KD):
                    split_fresh(fill_of[n] + k, c1(xhigh, k, T))
                {"cffn": ffn, "ffn": ffn, "attn": attn, "gmlp": gmlp}[ph[0]](n, ph)
            for tb in range(4):
                for half in range(2):
                    eng.wait_ge(store_turned, 2 * tb + half + 1)
                    eng.copy(otok[:, tb * D + half * 512:tb * D + half * 512 + 512],
                             misc[:, ((2 * tb + half) % 4) * 512:((2 * tb + half) % 4) * 512 + 512]
                             ).then_inc(store_copied, 1)

        @block.vector
        def _(eng):
            step = [0]

            def link(ins):
                step[0] += 1
                ins.then_inc(small_step, 1)
                eng.wait_ge(small_step, step[0])

            def small_parameters():
                lg = [par[:, COL[("hg_lb_logits", l, 0)]:COL[("hg_lb_logits", l, 0)] + 4] for l in L2]
                tmp = sm(S_TMP, 8)
                mx = sm(S_TMP + 8, 4)
                link(eng.tensor_tensor(mx, lg[0], lg[1], ALU.max))
                link(eng.tensor_tensor(sm(S_TMP, 4), lg[0], mx, ALU.subtract))
                link(eng.tensor_tensor(sm(S_TMP + 4, 4), lg[1], mx, ALU.subtract))
                assert step[0] == SMALL_AT[0]
                eng.wait_ge(small_act, 1)
                link(eng.tensor_tensor(mx, sm(S_TMP, 4), sm(S_TMP + 4, 4), ALU.add))
                link(eng.reciprocal(mx, mx))
                link(eng.tensor_tensor(sm(S_TMP, 4), sm(S_TMP, 4), mx, ALU.mult))
                link(eng.tensor_tensor(sm(S_TMP + 4, 4), sm(S_TMP + 4, 4), mx, ALU.mult))
                link(eng.tensor_tensor(sm(S_TMP + 4, 4), sm(S_TMP, 4), sm(S_TMP + 4, 4), ALU.add))
                link(eng.tensor_tensor(sm(S_LB, 4), sm(S_TMP, 4), sm(S_TMP, 4), ALU.subtract))
                link(eng.tensor_tensor(sm(S_LB + 4, 4), sm(S_TMP + 4, 4), sm(S_TMP, 4), ALU.subtract))
                link(eng.tensor_scalar(sm(S_OML, 8), sm(S_LB, 8), -1.0, 1.0, ALU.mult, ALU.add))
                link(eng.tensor_scalar(sm(S_OMLS, 8), sm(S_OML, 8), float(P) ** -0.5, None, ALU.mult))
                lam = small[:, S_TMP + 16:S_TMP + 20]
                y = sm(S_TMP + 8, 4)
                z = sm(S_TMP, 4)
                z2 = sm(S_TMP + 4, 4)
                for l in L2:
                    c = COL[("lru_lambda", l, 0)]
                    link(eng.tensor_copy(lam[:, 2 * l:2 * l + 2], par[:, c:c + 2]))
                link(eng.tensor_scalar(z, lam, -1.0, None, ALU.mult))
                link(eng.tensor_tensor(y, z, lam, ALU.min))
                assert step[0] == SMALL_AT[1], step[0]
                eng.wait_ge(small_act, 2)
                link(eng.tensor_scalar(sm(S_SP, 4), z, 0.0, None, ALU.max))
                link(eng.tensor_scalar(z, y, 2.0, None, ALU.add))
                link(eng.reciprocal(z, z))
                link(eng.tensor_tensor(z, z, y, ALU.mult))
                link(eng.tensor_tensor(z2, z, z, ALU.mult))
                terms = [1.0 / k for k in range(15, 1, -2)]
                link(eng.tensor_scalar(y, z2, terms[0], None, ALU.mult))
                for t in terms[1:]:
                    link(eng.scalar_tensor_tensor(out=y, in0=y, scalar=t, in1=z2, op0=ALU.add, op1=ALU.mult))
                link(eng.scalar_tensor_tensor(out=y, in0=y, scalar=1.0, in1=z, op0=ALU.add, op1=ALU.mult))
                link(eng.scalar_tensor_tensor(out=y, in0=y, scalar=2.0, in1=sm(S_SP, 4), op0=ALU.mult, op1=ALU.add))
                link(eng.tensor_scalar(sm(S_SP, 4), y, 8.0, None, ALU.mult))
                link(eng.tensor_scalar(sm(S_NSP, 4), y, -8.0, None, ALU.mult))
                link(eng.tensor_scalar(sm(S_GQ), pcol("attn_q_norm_2", 0), AD ** -0.5, None, ALU.mult))
                link(eng.tensor_scalar(sm(S_SUB), pcol("attn_subln_2", 0), 1.0 - LAM_INIT, None, ALU.mult))
                eng.wait_ge(lam_in, 64)
                for k in range(2):
                    x0, x1 = (lamv[:, (2 * k + i) * AD:(2 * k + i + 1) * AD] for i in range(2))
                    link(eng.tensor_tensor(x0, x0, x1, ALU.mult))
                    link(eng.tensor_reduce(sm(S_TMP + 12 + k), x0, AX.X, ALU.add))
                assert step[0] == SMALL_AT[2], step[0]
                eng.wait_ge(small_act, 3)
                link(eng.tensor_tensor(sm(S_NLAM), sm(S_TMP + 13), sm(S_TMP + 12), ALU.subtract))
                link(eng.tensor_scalar(sm(S_NLAM), sm(S_NLAM), LAM_INIT, None, ALU.subtract))

            def clear_sum(j, T):
                if j:
                    eng.wait_ge(ms_done, j)
                    eng.wait_ge(root_step, roots[0] * ROOT_STEPS)
                eng.memset(acc[:, 0:T], 0.0).then_inc(summed, 1)

            def add_squares(j, k, s, T):
                eng.wait_ge(squared, 8 * j + k + 1)
                eng.wait_ge(summed, 9 * j + 1 + k)
                eng.tensor_tensor(acc[:, 0:T], acc[:, 0:T], c1(sqr, s, T), ALU.add).then_inc(summed, 1)

            roots = [0]

            def root(dst, src, eps, done, tmp=acc, ahead=None):
                t = tmp[:, 0:dst.shape[-1]]
                at = ((0 if ahead is None else ahead) + roots[0]) * ROOT_STEPS
                bits = dst.bitcast(mybir.dt.int32)

                def step(m, ins):
                    ins.then_inc(root_step, 1)
                    eng.wait_ge(root_step, at + m + 1)
                step(0, eng.tensor_scalar(dst, src, eps, None, ALU.add))
                step(1, eng.tensor_scalar(bits, bits, -0.5, float(ROOT_BITS), ALU.mult, ALU.add))
                step(2, eng.scalar_tensor_tensor(out=t, in0=src, scalar=eps, in1=dst, op0=ALU.add, op1=ALU.mult))
                step(3, eng.tensor_tensor(t, t, dst, ALU.mult))
                step(4, eng.scalar_tensor_tensor(out=t, in0=t, scalar=ROOT_P, in1=t, op0=ALU.add, op1=ALU.mult))
                step(5, eng.scalar_tensor_tensor(out=dst, in0=t, scalar=ROOT_Q, in1=dst, op0=ALU.add, op1=ALU.mult))
                step(6, eng.scalar_tensor_tensor(out=t, in0=src, scalar=eps, in1=dst, op0=ALU.add, op1=ALU.mult))
                step(7, eng.scalar_tensor_tensor(out=t, in0=t, scalar=-0.5, in1=dst, op0=ALU.mult, op1=ALU.mult))
                eng.scalar_tensor_tensor(out=dst, in0=t, scalar=1.5, in1=dst, op0=ALU.add, op1=ALU.mult
                                         ).then_inc(done, 1)
                if ahead is None:
                    roots[0] += 1

            def give(q, write):
                if q >= 2:
                    eng.wait_ge(x_ready, q - 1)
                write(q % 2).then_inc(fresh_ready, 1)

            def split_low(q, high, low):
                eng.wait_ge(xhigh_ready, q + 1)
                n = high.shape[-1]
                eng.tensor_tensor(low, c1(fresh, q % 2, n), high.bitcast(F32), ALU.subtract).then_inc(x_ready, 1)

            def norm_root(j, T):
                eng.wait_ge(ms_done, j + 1)
                root(rcol[:, 0:len(blocks(T))], misc[:, 0:len(blocks(T))], EPS, rstd_ready, rcol2)
                eng.wait_ge(rstd_spread, j + 1)
                eng.tensor_copy(rstd[:, 0:T], by_block(misc, 0, T)).then_inc(rstd_wide, 1)
                eng.wait_ge(rstd_wide, j + 1)

            def norm(n, name, l):
                j, q0 = norm_of[n], fill_of[n]
                T = norm_T[j]
                norm_root(j, T)
                for k in range(KD + 1):
                    if k < KD:
                        give(q0 + k, lambda s: eng.scalar_tensor_tensor(
                            out=c1(fresh, s, T), in0=hc(k, T), scalar=pcol(name, l, k), in1=rstd[:, 0:T],
                            op0=ALU.mult, op1=ALU.mult))
                    if k:
                        split_low(q0 + k - 1, c1(xhigh, k - 1, T), c1(xlow, k - 1, T))

            clear_sum(0, T1)
            for k in range(KD):
                eng.wait_ge(x_turned, k + 1)
                eng.tensor_copy(hc(k), misc[:, (k % 2) * 1024 + 496:(k % 2) * 1024 + 1024]).then_inc(h_loaded, 1)
            for k in range(KD):
                add_squares(0, k, k % 2, T1)
            eng.wait_ge(par_turned, NROW_TILES)
            for n in range(NROW_TILES):
                eng.tensor_copy(par[:, n * P:(n + 1) * P], misc[:, n * P:(n + 1) * P]).then_inc(par_ready, 1)
            eng.wait_ge(par_ready, NROW_TILES)

            def residual(st, n, tile0, T, scale=None, bias=None, per_tile=1, last=True):
                more = last and norm_of[n] + 1 < norms
                if more:
                    clear_sum(norm_of[n] + 1, T)

                def body(i):
                    for s in range(2):
                        k = 2 * i + s
                        eng.wait_ge(slab_done, st.base + per_tile * (k + 1))
                        ps = wide(big, s, T)
                        if bias:
                            ins = eng.scalar_tensor_tensor(out=hc(k, T), in0=ps, scalar=bias(k), in1=hc(k, T),
                                                           op0=ALU.add, op1=ALU.add)
                        elif scale:
                            ins = eng.scalar_tensor_tensor(out=hc(k, T), in0=ps, scalar=scale, in1=hc(k, T),
                                                           op0=ALU.mult, op1=ALU.add)
                        else:
                            ins = eng.tensor_tensor(hc(k, T), ps, hc(k, T), ALU.add)
                        ins.then_inc(tile_out[s], 1)
                        if more:
                            add_squares(norm_of[n] + 1, k, s, T)
                repeat(eng, 0, KD // 2, body)

            def ffn(n, ph):
                conv = ph[0] == "cffn"
                T = T1 if conv else T2
                for half in range(2):
                    up, down = ph[2][2 * half:2 * half + 2]
                    tile0 = tile_of[n] + half * (2 * HF + KD)
                    first = FFN_AT[n] + half * HF

                    def body(i):
                        f = half * HF + i
                        if conv:
                            l = ph[1]
                            for s, z in enumerate((zg, zu)):
                                y = wide(big, s, T)
                                eng.wait_ge(z_ready, 2 * (first + i) + s + 1)
                                eng.scalar_tensor_tensor(
                                    out=z[:, 1:T], in0=y[:, 0:T - 1],
                                    scalar=pdyn("ffn_conv_w", l, 2 * NF + s * NF + f), in1=z[:, 1:T],
                                    op0=ALU.mult, op1=ALU.add).then_inc(conv_step, 1)
                                eng.wait_ge(conv_step, 2 * (first + i) + s + 1)
                                eng.scalar_tensor_tensor(
                                    out=z[:, 2:T], in0=y[:, 0:T - 2], scalar=pdyn("ffn_conv_w", l, s * NF + f),
                                    in1=z[:, 2:T], op0=ALU.mult, op1=ALU.add).then_inc(tile_out[s], 1)
                            eng.wait_ge(tile_out[1], tile0 // 2 + i + 1)
                            eng.wait_ge(silu_ready, first + i + 1)
                            val = zu[:, :]
                        else:
                            eng.wait_ge(tile_out[0], tile0 // 2 + i + 1)
                            eng.wait_ge(slab_done, up.base + 2 * i + 2)
                            val = wide(big, 1, T)
                        if not (isinstance(i, int) and first + i == 0):
                            eng.wait_ge(hid_ready, first + i)
                        made = (prod_ready, first + i + 1) if conv else (tile_out[1], tile0 // 2 + i + 1)
                        eng.tensor_tensor(pr[:, 0:T], sg[:, 0:T], val, ALU.mult).then_inc(made[0], 1)
                        eng.wait_ge(*made)
                        eng.tensor_copy(c1(hidh, i, T), pr[:, 0:T]).then_inc(hidh_ready, 1)
                        eng.wait_ge(hidh_ready, first + i + 1)
                        eng.tensor_tensor(c1(hidl, i, T), pr[:, 0:T], c1(hidh, i, T).bitcast(F32),
                                          ALU.subtract).then_inc(hid_ready, 1)
                    body(0)
                    repeat(eng, 1, HF, body)
                    residual(down, n, tile0 + 2 * HF, T, scale=None if conv else 0.5, last=half == 1)

            def mix(n, ph):
                l, first, wout = ph[1], ph[2], ph[3]
                s0, t0, q0 = first.base, tile_of[n], fill_of[n]

                def tile_wait(i):
                    eng.wait_ge(tile_out[i % 2], (t0 + i) // 2 + 1)

                eng.memset(lx[:, :].rearrange("p (c t) -> p c t", c=2)[:, :, 0:TAPS - 1], 0.0).then_inc(pad_zero.sem, 1)
                for i in range(HH):
                    tile_wait(TILE_HF + i)
                    eng.tensor_scalar(c1(logf, i), c1(logf, i), sm(S_OML + 4 * l + i), F_MIN, ALU.mult, ALU.max)
                    eng.tensor_scalar(c1(kk, i), c1(kk, i), sm(S_OMLS + 4 * l + i), None, ALU.mult
                                      ).then_inc(fk_ready.sem, 1)
                one = square("one")
                eng.wait_ge(x_ready, q0 + KD)

                def prep(c):
                    tk, w = CHUNKS[c]
                    levels = LEVELS[c > 0]
                    g0 = steps.index((l, c, 0))
                    b = bcum[:, 0:4 * w]
                    if c:
                        eng.wait_ge(exp_ready.sem, exp_ready.at(l, c - 1, 0))
                        eng.wait_ge(decay_ready.sem, decay_ready.at(l, c - 1, 1 + len(LEVELS[c > 1])))
                    for i in range(HH):
                        ins = eng.tensor_tensor_scan(b[:, i * w:(i + 1) * w], one[:, 0:w],
                                                     logf[:, i * T1 + tk:i * T1 + tk + w], 0.0, ALU.mult, ALU.add)
                    ins.then_inc(scanned.sem, 1)
                    eng.wait_ge(scanned.sem, scanned.at(l, c))

                    def cut(t, two=None, r=None):
                        x = t[:, :].rearrange("p (i t) -> p i t", i=HH)[:, :, tk:tk + w]
                        return x.rearrange("p i (g two r) -> p i g two r", two=2, r=r) if two else x

                    def exponent(j):
                        g = g0 + j
                        if g >= 2:
                            eng.wait_ge(exp_ready.sem, g - 1)
                        r = w if j == 1 else 2 * levels[j - 2]
                        ref = (w if j == 1 else levels[j - 2]) - 1
                        x = xlev[:, (g % 2) * T1:(g % 2) * T1 + 4 * w].rearrange("p (g r) -> p g r", r=r)
                        bv = b.rearrange("p (g r) -> p g r", r=r)
                        eng.tensor_tensor(x, bv, bv[:, :, ref:ref + 1].to_broadcast([P, 4 * w // r, r]),
                                          ALU.subtract).then_inc(decay_ready.sem, 1)

                    def product(j):
                        g = g0 + j
                        e = elev[:, (g % 2) * T1:(g % 2) * T1 + 4 * w]
                        eng.wait_ge(exp_ready.sem, g + 1)
                        e4 = e.rearrange("p (i t) -> p i t", i=HH)
                        if j < 2:
                            dst, src = ((qdec, q), (kdec, kk))[j]
                            eng.tensor_tensor(dst[:, 0:4 * w].rearrange("p (i t) -> p i t", i=HH), cut(src), e4,
                                              ALU.mult).then_inc(lev_ready.sem, 1)
                            return
                        r = levels[j - 2]
                        dst = lev[:, (j - 2) * 512:(j - 2) * 512 + 4 * w].rearrange(
                            "p (i g two r) -> p i g two r", i=HH, two=2, r=r)
                        e5 = e.rearrange("p (i g two r) -> p i g two r", i=HH, two=2, r=r)
                        for half, src in enumerate((kk, q)):
                            ins = eng.tensor_tensor(dst[:, :, :, half, :], cut(src, True, r)[:, :, :, half, :],
                                                    e5[:, :, :, half, :], ALU.mult)
                        ins.then_inc(lev_ready.sem, 1)

                    n_steps = 2 + len(levels)
                    for j in range(1, n_steps + 1):
                        if j < n_steps:
                            exponent(j)
                        if j == 1:
                            if c:
                                eng.wait_ge(headout.sem, headout.at(l, c - 1, HH - 1))
                            for i in range(HH):
                                tile_wait(TILE_HQ + i)
                        product(j - 1)

                def heads(c):
                    tk, w = CHUNKS[c]
                    mw = LM1 if c else LM0
                    mask = level_masks[0:w, LM0:LM0 + LM1] if c else level_masks[0:w, 0:LM0]
                    for i in range(HH):
                        k = scored.at(l, c, i)
                        eng.wait_ge(scored.sem, k)
                        if k > 2:
                            eng.wait_ge(headout.sem, k - 2)
                        eng.tensor_tensor(psc[i % 2][0:w, 0:mw], misc[0:w, (2 + i % 2) * BANK:(2 + i % 2) * BANK + mw],
                                          mask, ALU.mult).then_inc(masked.sem, 1)
                    if c < len(CHUNKS) - 1:
                        eng.wait_ge(upd_done.sem, upd_done.at(l, c))
                        if c == 0:
                            eng.tensor_copy(state[:, :], misc[:, BANK:2 * BANK]).then_inc(state_ready.sem, 1)
                        else:
                            eng.wait_ge(state_ready.sem, state_ready.at(l, c - 1))
                            for i in range(HH):
                                s_i = state[:, i * P:(i + 1) * P]
                                ins = eng.scalar_tensor_tensor(
                                    out=s_i, in0=s_i, scalar=fend[:, 4 * (c % 2) + i:4 * (c % 2) + i + 1],
                                    in1=misc[:, BANK + i * P:BANK + (i + 1) * P], op0=ALU.mult, op1=ALU.add)
                            ins.then_inc(state_ready.sem, 1)

                eng.wait_ge(logf_ready.sem, logf_ready.at(l))
                for what, x in MIX_ORDER:
                    if what == "prep":
                        prep(x)
                    elif what == "heads":
                        heads(x)

                for p in range(2):
                    eng.wait_ge(cv_start.sem, cv_start.at(l, p))
                    for m in range(TAPS - 1):
                        if m:
                            eng.wait_ge(cv_step.sem, cv_step.at(l, p, m - 1))
                        eng.scalar_tensor_tensor(out=c1(cv, p), in0=lx[:, p * XP + m:p * XP + m + T1],
                                                 scalar=pcol("lru_conv_w", l, 2 * m + p), in1=c1(cv, p),
                                                 op0=ALU.mult, op1=ALU.add).then_inc(cv_step.sem, 1)
                qq = q0 + KD
                eng.wait_ge(oms_done.sem, oms_done.at(l))
                root(rcol[:, 0:20], misc[:, 0:20], EPS, orstd.sem, rcol2)
                eng.wait_ge(gates_ready.sem, gates_ready.at(l, "hg"))
                eng.wait_ge(slab_done, s0 + MIX_TILES)
                for i in range(HH + 1):
                    if i < HH:
                        eng.wait_ge(ospread.sem, ospread.at(l, i))
                        eng.scalar_tensor_tensor(out=c1(q, i), in0=c1(q, i), scalar=pcol("hg_norm_g", l),
                                                 in1=by_block(misc, i % 2, T1), op0=ALU.mult, op1=ALU.mult).then_inc(oscaled.sem, 1)
                        eng.wait_ge(oscaled.sem, oscaled.at(l, i))
                        give(qq + i, lambda s: eng.tensor_tensor(c1(fresh, s), c1(q, i), c1(hg_gate, i), ALU.mult))
                    if i:
                        split_low(qq + i - 1, c1(xhigh, i - 1), c1(xlow, i - 1))

                for x, (t, name) in enumerate(((rq, "q"), (rk, "k"))):
                    cos, sin = (rotary[:, (2 * x + y) * T1:(2 * x + y + 1) * T1] for y in range(2))
                    eng.wait_ge(rotated.sem, rotated.at(l, name))
                    if x:
                        eng.wait_ge(rope_step.sem, rope_step.at(l, "q", 2))
                    eng.tensor_tensor(rtmp[:, :], wide(misc, x, T1), sin, ALU.mult).then_inc(rope_step.sem, 1)
                    eng.tensor_tensor(t[:, :], t[:, :], cos, ALU.mult).then_inc(rope_step.sem, 1)
                    eng.wait_ge(rope_step.sem, rope_step.at(l, name, 1))
                    eng.tensor_tensor(t[:, :], t[:, :], rtmp[:, :], ALU.add).then_inc(rope_step.sem, 1)
                def recurrence(p, part):
                    A, TH, I = c1(la, p), c1(lt, p), c1(li, p)

                    def chain(m, ins):
                        ins.then_inc(lru_step.sem, 1)
                        eng.wait_ge(lru_step.sem, lru_step.at(l, p, m))
                    if part == 0:
                        eng.wait_ge(lru_exp.sem, lru_exp.at(l, p))
                        chain(0, eng.tensor_tensor(c1(lh, p), A, A, ALU.mult))
                        chain(1, eng.scalar_tensor_tensor(out=TH, in0=c1(lh, p), scalar=1.0, in1=TH,
                                                          op0=ALU.add, op1=ALU.mult))
                        chain(2, eng.tensor_scalar(TH, TH, 0.0, None, ALU.max))
                        chain(3, eng.tensor_tensor(I, I, c1(cv, p), ALU.mult))
                    else:
                        eng.wait_ge(lru_root.sem, lru_root.at(l, p))
                        chain(4, eng.tensor_tensor(I, I, TH, ALU.mult))
                        chain(5, eng.tensor_tensor_scan(c1(lh, p), A, I, 0.0, ALU.mult, ALU.add))

                for i in range(RH):
                    for c, (tk, w) in enumerate(CHUNKS):
                        u = units.index((l, i, c))
                        sl = u % 2
                        if (i, c) in LRU_AT:
                            recurrence(*LRU_AT[i, c])
                        eng.wait_ge(rscored.sem, u + 1)
                        if u >= 2:
                            eng.wait_ge(rapplied.sem, u - 1)
                        eng.tensor_tensor(rp[0:w, sl * T1:sl * T1 + w],
                                          misc[0:w, sl * 1024 + 496 + tk:sl * 1024 + 496 + tk + w],
                                          square("causal", w, w), ALU.mult).then_inc(rdiag.sem, 1)
                for p in range(2):
                    eng.wait_ge(rmean.sem, rmean.at(l, p))
                    eng.tensor_tensor(c1(ro, p), c1(ro, p), wide(misc, p, T1), ALU.subtract).then_inc(rcentred.sem, 1)
                eng.wait_ge(gates_ready.sem, gates_ready.at(l, "ret"))
                eng.wait_ge(rvar.sem, rvar.at(l))
                root(rcol[:, 0:20], misc[:, 0:20], EPS, rrstd.sem, rcol2)
                for p in range(3):
                    if p < 2:
                        eng.wait_ge(rspread.sem, rspread.at(l, p))
                        eng.scalar_tensor_tensor(out=c1(ro, p), in0=c1(ro, p), scalar=pcol("ret_norm_g", l),
                                                 in1=by_block(misc, p, T1), op0=ALU.mult, op1=ALU.mult
                                                 ).then_inc(rnormed.sem, 1)
                        eng.wait_ge(rnormed.sem, rnormed.at(l, p))
                        give(qq + 4 + p, lambda s: eng.tensor_tensor(c1(fresh, s), c1(ro, p), c1(ret_gate, p), ALU.mult))
                    if p:
                        split_low(qq + 3 + p, c1(xhigh, 3 + p), c1(xlow, 3 + p))

                eng.wait_ge(gates_ready.sem, gates_ready.at(l, "lru"))
                for p in range(3):
                    if p < 2:
                        give(qq + 6 + p, lambda s: eng.tensor_tensor(c1(fresh, s), c1(lh, p), c1(lru_gate, p), ALU.mult))
                    if p:
                        split_low(qq + 5 + p, c1(xhigh, 5 + p), c1(xlow, 5 + p))
                residual(wout, n, t0 + MIX_TILES, T1)

            def attn(n, ph):
                win, wout = ph[2], ph[3]
                s0, t0, q0 = win.base, tile_of[n], fill_of[n]
                for x, gain in enumerate((sm(S_GQ), pcol("attn_k_norm_2", 0))):
                    def body(i):
                        for s in range(2):
                            k = 8 * x + 2 * i + s
                            eng.wait_ge(qms_done, k + 1)
                            if not isinstance(k, int) or k:
                                eng.wait_ge(qn_ready, k)
                            root(rstd[:, 0:T2], misc[:, s * 1024:s * 1024 + T2], EPS, qrstd, ahead=k)
                            eng.wait_ge(qrstd, k + 1)
                            eng.scalar_tensor_tensor(out=c2(qkv, k), in0=c2(qkv, k), scalar=gain, in1=rstd[:, 0:T2],
                                                     op0=ALU.mult, op1=ALU.mult).then_inc(qn_ready, 1)
                    body(0)
                    repeat(eng, 1, 4, body)
                roots[0] += 16

                def maxima(u):
                    b = u % 4
                    L = (b + 1) * P
                    sl = u % 2
                    sc = misc[:, sl * 1024:sl * 1024 + 1024].rearrange("p (c k) -> p c k", c=2)
                    eng.wait_ge(ascored, u + 1)
                    dg = sc[:, :, b * P:(b + 1) * P]
                    eng.tensor_tensor(dg, dg, square("future").unsqueeze(1).to_broadcast([P, 2, P]), ALU.add
                                      ).then_inc(amasked, 1)
                    eng.wait_ge(amasked, u + 1)
                    if u >= 2:
                        eng.wait_ge(aexp_ready, u - 1)
                    eng.tensor_reduce(stat[:, 2 * sl:2 * sl + 2], sc[:, :, 0:L], AX.X, ALU.max, negate=True
                                      ).then_inc(amax_ready, 1)

                def combine(u):
                    L = (u % 4 + 1) * P
                    sl = u % 2
                    den = stat[:, 4 + 2 * sl:6 + 2 * sl]
                    rec = stat[:, 8 + 2 * sl:10 + 2 * sl]
                    eng.wait_ge(aexp_ready, u + 1)
                    eng.reciprocal(rec, den).then_inc(astep, 1)
                    eng.wait_ge(astep, 3 * u + 1)
                    eng.tensor_scalar(rec[:, 1:2], rec[:, 1:2], sm(S_NLAM), None, ALU.mult).then_inc(astep, 1)
                    eng.wait_ge(astep, 3 * u + 2)
                    if u >= 2:
                        eng.wait_ge(aturned, 5 * ((u - 2) // 4) + (u - 2) % 4 + 2)
                    A = c2(aa, sl, L)
                    eng.tensor_scalar(A, ex[:, sl * 1024 + 512:sl * 1024 + 512 + L], rec[:, 1:2], None, ALU.mult
                                      ).then_inc(astep, 1)
                    eng.wait_ge(astep, 3 * u + 3)
                    eng.scalar_tensor_tensor(out=A, in0=ex[:, sl * 1024:sl * 1024 + L], scalar=rec[:, 0:1], in1=A,
                                             op0=ALU.mult, op1=ALU.add).then_inc(a_ready, 1)

                def out_root(m):
                    at0 = 1024 + (m % 2) * 512
                    eng.wait_ge(aoms, m + 1)
                    if m:
                        eng.wait_ge(aospread, m)
                    root(rcol[:, 0:4], big[:, at0:at0 + 4], EPS, aorstd, rcol2)

                def out_norm(m):
                    eng.wait_ge(aospread, m + 1)
                    give(q0 + KD + m, lambda s: eng.scalar_tensor_tensor(
                        out=c1(fresh, s, T2), in0=c2(oa, m % 2), scalar=sm(S_SUB),
                        in1=big[:, 1024 + (m % 2) * 512:1536 + (m % 2) * 512],
                        op0=ALU.mult, op1=ALU.mult))

                eng.wait_ge(slab_done, s0 + 24)
                eng.wait_ge(qn_ready, 16)
                maxima(0)
                for u in range(32):
                    m, b = u // 4, u % 4
                    if u + 1 < 32:
                        maxima(u + 1)
                    combine(u)
                    if b == 1 and m:
                        out_root(m - 1)
                    if b == 2 and m:
                        out_norm(m - 1)
                    if b == 3 and m:
                        split_low(q0 + KD + m - 1, c1(xhigh, m - 1, T2), c1(xlow, m - 1, T2))
                out_root(7)
                out_norm(7)
                split_low(q0 + KD + 7, c1(xhigh, 7, T2), c1(xlow, 7, T2))
                residual(wout, n, t0 + 24, T2)

            def gmlp(n, ph):
                sv, su, so = ph[2:]
                t0, q0 = tile_of[n], fill_of[n]
                for g in range(8):
                    eng.wait_ge(ws_turned, g + 1)
                    eng.tensor_tensor(wt[:, g * P:(g + 1) * P], misc[:, (g % 2) * 1024:(g % 2) * 1024 + P],
                                      square("causal"), ALU.mult).then_inc(ws_ready, 1)
                eng.wait_ge(ms_done, norm_of[n] + 1)
                eng.memset(acc[:, 0:T2], 0.0).then_inc(g_sum, 1)

                def vsum(i):
                    for s in range(2):
                        eng.wait_ge(tile_out[s], t0 // 2 + i + 1)
                        eng.wait_ge(g_sum, 2 * i + s + 1)
                        eng.tensor_tensor(acc[:, 0:T2], acc[:, 0:T2], c2(vv, 2 * i + s), ALU.add).then_inc(g_sum, 1)
                repeat(eng, 0, NG // 2, vsum)
                eng.wait_ge(g_stat, 1)
                eng.tensor_scalar(rstd[:, 0:T2], misc[:, 0:T2], D / GH, None, ALU.mult).then_inc(g_statv, 1)
                eng.wait_ge(g_statv, 1)
                eng.memset(acc[:, 0:T2], 0.0).then_inc(g_sum, 1)
                for m in range(NG + 1):
                    if m < NG:
                        eng.tensor_tensor(c2(vv, m), c2(vv, m), rstd[:, 0:T2], ALU.subtract).then_inc(g_centred, 1)
                    if m:
                        eng.wait_ge(g_sq, m)
                        eng.wait_ge(g_sum, 1 + NG + m)
                        eng.tensor_tensor(acc[:, 0:T2], acc[:, 0:T2], c1(sqr, (m - 1) % 2, T2), ALU.add
                                          ).then_inc(g_sum, 1)
                eng.wait_ge(g_stat, 2)
                eng.wait_ge(g_centred, NG)
                eng.tensor_scalar(c1(sqr, 0, T2), misc[:, 0:T2], D / GH, None, ALU.mult).then_inc(g_statv, 1)
                eng.wait_ge(g_statv, 2)
                root(rstd[:, 0:T2], c1(sqr, 0, T2), LN_EPS, g_statv)
                eng.wait_ge(g_statv, 3)
                for m in range(NG):
                    eng.tensor_tensor(c2(vv, m), c2(vv, m), rstd[:, 0:T2], ALU.mult).then_inc(g_scaled, 1)
                eng.wait_ge(slab_done, su.base + NG)
                for k in range(2):
                    eng.wait_ge(tile_out[k], (t0 + 2 * NG) // 2)
                eng.wait_ge(g_scaled, NG)
                tmp2 = (acc, rstd)
                for m in range(NG + 1):
                    if m < NG:
                        eng.wait_ge(g_mixed, m + 1)
                        if m >= 2:
                            eng.wait_ge(fresh_ready, q0 + KD + m - 1)
                        t = tmp2[m % 2][:, 0:T2]
                        g = m // 2
                        eng.tensor_tensor(t.rearrange("p (b t) -> p b t", t=P),
                                          misc[:, (m % 2) * 1024 + 512:(m % 2) * 1024 + 1024].rearrange("p (b t) -> p b t", t=P),
                                          bs[:, g * P:(g + 1) * P].unsqueeze(1).to_broadcast([P, 4, P]),
                                          ALU.add).then_inc(g_step, 1)
                        eng.wait_ge(g_step, m + 1)
                        give(q0 + KD + m, lambda s: eng.tensor_tensor(c1(fresh, s, T2), t, c2(uu, m), ALU.mult))
                    if m:
                        k = m - 1
                        hi = c1(xhigh, k, T2) if k < KD else c2(g2h, k - KD)
                        lo = c1(xlow, k, T2) if k < KD else c2(g2l, k - KD)
                        split_low(q0 + KD + k, hi, lo)
                residual(so, n, t0 + 2 * NG, T2, bias=lambda k: pdyn("gmlp_b_out_2", 0, k), per_tile=2)

            names = {"mix": "norm_mix_g", "cffn": "norm_ffn_g"}
            for n, ph in enumerate(plan):
                if ph[0] == "final":
                    norm_root(norm_of[n], T1)
                    more = norm_of[n] + 1 < norms
                    if more:
                        clear_sum(norm_of[n] + 1, T2)
                    for k in range(KD):
                        eng.scalar_tensor_tensor(out=hc(k, T2), in0=hc(k, T2), scalar=pcol("final_norm_g", None, k),
                                                 in1=rstd[:, META:T1], op0=ALU.mult, op1=ALU.mult).then_inc(final_done, 1)
                        if k and more:
                            add_squares(norm_of[n] + 1, k - 1, (k - 1) % 2, T2)
                    if more:
                        add_squares(norm_of[n] + 1, KD - 1, 1, T2)
                    continue
                if ph[0] == "ffn":
                    norm(n, f"ffn{ph[1] % 2 + 1}_norm_2", ph[1] // 2)
                elif ph[0] in ("attn", "gmlp"):
                    norm(n, "mix_norm_2", 0 if ph[0] == "attn" else 1)
                else:
                    norm(n, names[ph[0]], ph[1])
                if n == 0:
                    small_parameters()
                {"mix": mix, "cffn": ffn, "ffn": ffn, "attn": attn, "gmlp": gmlp}[ph[0]](n, ph)

        @block.tensor
        def _(eng):
            ident = square("identity")

            def slab(s, kc, xh, xl, T, slot, x0=0, width=T1, start=True, stop=True, before=None):
                for k in range(kc):
                    if before:
                        before(k)
                    for y, (w, x) in enumerate(((whigh, xh), (whigh, xl), (wlow, xh))):
                        for c, n in parts(T):
                            mm = eng.matmul(wide(big, slot, T)[:, c:c + n],
                                            w[:, (s * KC + k) * P:(s * KC + k + 1) * P],
                                            x[:, (x0 + k) * width + c:(x0 + k) * width + c + n],
                                            start=start and k == 0 and y == 0,
                                            stop=stop and k == kc - 1 and y == 2)
                mm.then_inc(slab_done, 1)

            def slab_ready(n):
                eng.wait_ge(slab_split, n + 1)

            def slot_free(s, t2):
                if not isinstance(t2, int) or t2 >= 1:
                    eng.wait_ge(tile_out[s], t2)

            def plain_pair(st, tile0, i, T, xh=None, xl=None, before=None, width=T1):
                for s in range(2):
                    slab_ready(st.base + 2 * i + s)
                    slot_free(s, tile0 // 2 + i)
                    slab(s, st.kc, xh or xhigh, xl or xlow, T, s, width=width,
                         before=before if s == 0 else None)

            def first_pair(st, tile0, T, q0, width=T1):
                for s in range(2):
                    slab_ready(st.base + s)
                    slot_free(s, tile0 // 2)
                for step in range(KD + LAG):
                    if step < KD:
                        eng.wait_ge(x_ready, q0 + step + 1)
                    for s, k in ((0, step), (1, step - LAG)):
                        if not 0 <= k < KD:
                            continue
                        for y, (w, x) in enumerate(((whigh, xhigh), (whigh, xlow), (wlow, xhigh))):
                            for c, n in parts(T):
                                mm = eng.matmul(wide(big, s, T)[:, c:c + n],
                                                w[:, (s * KC + k) * P:(s * KC + k + 1) * P],
                                                x[:, k * width + c:k * width + c + n],
                                                start=k == 0 and y == 0, stop=k == KD - 1 and y == 2)
                        if k == KD - 1:
                            mm.then_inc(slab_done, 1)

            def operand(q0):
                return lambda k: eng.wait_ge(x_ready, q0 + k + 1)

            def column_means(dst, col, mat, src, T, heads=1):
                for j, (x0, _, _) in enumerate(blocks(T)):
                    mm = eng.matmul(dst[:, col + j * heads:col + (j + 1) * heads], src[:, x0:x0 + P],
                                    square(mat)[:, 0:P:P // heads], start=True, stop=True)
                return mm

            def row_spread(dst, slot, col, T, heads=1):
                for j, (_, lo, w) in enumerate(blocks(T)):
                    at0 = slot * 1024 + (496 if T == T1 else 0)
                    for i in range(heads):
                        r = P // heads
                        c = col + j * heads + i
                        mm = eng.matmul(dst[i * r:(i + 1) * r, at0 + lo:at0 + lo + w],
                                        rcol[:, c:c + 1].to_broadcast([P, r]), square("identity", P, w),
                                        start=True, stop=True)
                return mm

            def norm_sum(j):
                T = norm_T[j]
                eng.wait_ge(summed, 9 * (j + 1))
                column_means(misc, 0, "mean1024", acc, T).then_inc(ms_done, 1)
                eng.wait_ge(rstd_ready, j + 1)
                row_spread(misc, 0, 0, T).then_inc(rstd_spread, 1)

            def spread(dst, mat, src, T):
                for c, n in parts(T):
                    mm = eng.matmul(dst[:, c:c + n], mat, src[:, c:c + n], start=True, stop=True)
                return mm

            eng.wait_ge(squares_in, 16)
            for j in range(5):
                eng.wait_ge(x_in[j], 16)
            for k in range(KD):
                at0 = (k % 2) * 1024 + 496
                if k >= 2:
                    eng.wait_ge(h_loaded, k - 1)
                eng.matmul(misc[:, at0:at0 + META], xin[0:META, k * P:(k + 1) * P], square("identity", META, META),
                           start=True, stop=True)
                for j in range(4):
                    mm = eng.transpose(misc[:, at0 + META + P * j:at0 + META + P * (j + 1)],
                                       xin[:, (j + 1) * D + k * P:(j + 1) * D + (k + 1) * P], ident)
                mm.then_inc(x_turned, 1)
            eng.wait_ge(par_in, 16 * len(par_loads[0::3] + par_loads[1::3]))
            eng.wait_ge(par_in_soft, 16 * len(par_loads[2::3]))
            eng.wait_ge(h_loaded, KD)
            for n in range(NROW_TILES):
                rows = min(P, len(ROWS) - n * P)
                eng.matmul(misc[:, n * P:(n + 1) * P], rowt[0:rows, n * P:(n + 1) * P], square("identity", rows, P),
                           start=True, stop=True).then_inc(par_turned, 1)
            eng.wait_ge(par_ready, NROW_TILES)
            eng.wait_ge(tab_in, 32)

            def ffn(n, ph):
                T = T1 if ph[0] == "cffn" else T2
                for half in range(2):
                    up, down = ph[2][2 * half:2 * half + 2]
                    tile0 = tile_of[n] + half * (2 * HF + KD)
                    if half == 0:
                        first_pair(up, tile0, T, fill_of[n])
                    else:
                        plain_pair(up, tile0, 0, T)
                    repeat(eng, 1, HF, lambda i: plain_pair(up, tile0, i, T))
                    first = FFN_AT[n] + half * HF
                    tile0 += 2 * HF
                    plain_pair(down, tile0, 0, T, hidh, hidl, before=lambda k: eng.wait_ge(hid_ready, first + k + 1))
                    repeat(eng, 1, KD // 2, lambda i: plain_pair(down, tile0, i, T, hidh, hidl))

            def mix(n, ph):
                l, first, wout = ph[1], ph[2], ph[3]
                s0, t0, q0 = first.base, tile_of[n], fill_of[n]

                def tile_wait(i):
                    eng.wait_ge(tile_out[i % 2], (t0 + i) // 2 + 1)

                def tile(i):
                    slab_ready(s0 + i)
                    slot_free(i % 2, (t0 + i) // 2)
                    slab(i % 2, KD, xhigh, xlow, T1, i % 2)

                def heads(c):
                    tk, w = CHUNKS[c]
                    levels = LEVELS[c > 0]
                    eng.wait_ge(lev_ready.sem, lev_ready.at(l, c, 1 + len(levels)))
                    for i in range(HH):
                        tile_wait(TILE_HI + i)
                    if c:
                        eng.wait_ge(o_ready.sem, o_ready.at(l, c - 1))
                        eng.wait_ge(state_ready.sem, state_ready.at(l, c - 1))
                    for t, name, at0 in ((v, "v", 0), (kdec, "k", BANK)):
                        for i in range(HH):
                            src = t[:, i * T1 + tk:i * T1 + tk + w] if name == "v" else t[:, i * w:(i + 1) * w]
                            dst = misc[0:w, at0 + i * P:at0 + (i + 1) * P]
                            mm = eng.transpose(dst, src, ident) if w == P else eng.matmul(
                                dst, src, ident, start=True, stop=True)
                        mm.then_inc(turned.sem, 1)

                    def score(i):
                        bank = misc[0:w, (2 + i % 2) * BANK:(3 + i % 2) * BANK]
                        mm = eng.matmul(bank[:, 0:w], kk[:, i * T1 + tk:i * T1 + tk + w],
                                        q[:, i * T1 + tk:i * T1 + tk + w], start=True, stop=True)
                        col = w
                        for k, r in enumerate(levels):
                            if r == 64:
                                continue
                            m = lev[:, k * 512 + i * w:k * 512 + (i + 1) * w]
                            mm = eng.matmul(bank[:, col:col + w // 2], m,
                                            m.rearrange("p (g two r) -> p g two r", two=2, r=r)[:, :, 1, :],
                                            start=True, stop=True)
                            col += w // 2
                        mm.then_inc(scored.sem, 1)

                    def apply(i):
                        o = misc[:, i * P:i * P + w]
                        vt = vtok[0:w, i * P:(i + 1) * P]
                        pm = psc[i % 2][0:w, :]
                        eng.matmul(o, vt, pm[:, 0:w], start=True, stop=False, skip_group_check=True)
                        col = w
                        for r in levels:
                            if r == 64:
                                eng.matmul(o[:, 64:128], vtok[0:64, i * P:(i + 1) * P], p64[0:64, i * 64:(i + 1) * 64],
                                           start=False, stop=False, skip_group_check=True)
                                continue
                            mm = eng.matmul(o.rearrange("p (g two r) -> p g two r", two=2, r=r)[:, :, 1, :], vt,
                                            pm[:, col:col + w // 2], start=False, stop=r == 1 and c == 0,
                                            skip_group_check=True)
                            col += w // 2
                        if c:
                            mm = eng.matmul(o, state[:, i * P:(i + 1) * P], qdec[:, i * w:(i + 1) * w],
                                            start=False, stop=True, skip_group_check=True)
                        mm.then_inc(headout.sem, 1)

                    for i in range(2):
                        k = scored.at(l, c, i)
                        if k > 2:
                            eng.wait_ge(masked.sem, k - 2)
                        score(i)
                    eng.wait_ge(tok_ready.sem, tok_ready.at(l, c, "k"))
                    if c:
                        for i in range(HH):
                            m = lev[:, i * w:(i + 1) * w]
                            mm = eng.matmul(misc[0:64, BANK + i * 64:BANK + (i + 1) * 64], m[:, 0:64], m[:, 64:128],
                                            start=True, stop=True)
                        mm.then_inc(scored64.sem, 1)
                    for i in range(HH):
                        eng.wait_ge(masked.sem, masked.at(l, c, i))
                        if c and i == 0:
                            eng.wait_ge(p64_ready.sem, p64_ready.at(l, c))
                        apply(i)
                        if i + 2 < HH:
                            score(i + 2)
                    if c < len(CHUNKS) - 1:
                        for i in range(HH):
                            mm = eng.matmul(misc[:, BANK + i * P:BANK + (i + 1) * P], ktok[0:w, i * P:(i + 1) * P],
                                            vtok[0:w, i * P:(i + 1) * P], start=True, stop=True)
                        mm.then_inc(upd_done.sem, 1)

                first_pair(first, t0, T1, q0)
                for i in range(2, 12):
                    tile(i)
                for what, x in MIX_ORDER:
                    if what == "slab":
                        tile(x)
                    elif what == "heads":
                        heads(x)

                eng.wait_ge(osq_ready.sem, osq_ready.at(l))
                for i in range(HH):
                    mm = column_means(misc, 5 * i, "mean128", c1(kk, i), T1)
                mm.then_inc(oms_done.sem, 1)
                eng.wait_ge(gatew_in, 16 * 8)
                for s in range(2):
                    tile_wait(MIX_TILES - 2 + s)
                for p in range(2):
                    eng.wait_ge(cv_step.sem, cv_step.at(l, p, TAPS - 2))
                    for x in range(2):
                        if p:
                            eng.wait_ge(gsig.sem, gsig.at(l, p - 1, "ai"[x]))
                        w0 = ((l * 2 + x) * 2 + p) * P
                        spread(wide(big, x, T1), gatew[:, w0:w0 + P], c1(cv, p), T1).then_inc(gated.sem, 1)
                eng.wait_ge(orstd.sem, orstd.at(l))
                for i in range(HH):
                    if i >= 2:
                        eng.wait_ge(oscaled.sem, oscaled.at(l, i - 2))
                    row_spread(misc, i % 2, 5 * i, T1).then_inc(ospread.sem, 1)
                for x, t in enumerate((rq, rk)):
                    eng.wait_ge(oscaled.sem, oscaled.at(l, 2 + x))
                    spread(wide(misc, x, T1), square("rotate"), t, T1).then_inc(rotated.sem, 1)
                eng.wait_ge(gsig.sem, gsig.at(l, 1, "i"))
                for c, (tk, w) in enumerate(CHUNKS):
                    for p in range(2):
                        dst = big[0:w, c * 256 + p * P:c * 256 + (p + 1) * P]
                        src = rv[:, p * T1 + tk:p * T1 + tk + w]
                        mm = eng.transpose(dst, src, ident) if w == P else eng.matmul(
                            dst, src, ident, start=True, stop=True)
                mm.then_inc(rvturned.sem, 1)

                def rscore(u):
                    _, i, c = units[u]
                    tk, w = CHUNKS[c]
                    sl = u % 2
                    if u % 20 >= 2:
                        eng.wait_ge(rdiag.sem, u - 1)
                        if units[u - 2][2] < len(CHUNKS) - 1:
                            eng.wait_ge(rrest.sem, rrest.at(*units[u - 2]))
                    rows = slice(RDK * i, RDK * (i + 1))
                    spans = [(0, META), (META, T1)] if c == 0 else [(tk, T1)]
                    for lo, hi in spans:
                        mm = eng.matmul(misc[0:w, sl * 1024 + 496 + lo:sl * 1024 + 496 + hi],
                                        rk[rows, tk:tk + w], rq[rows, lo:hi], start=True, stop=True)
                    mm.then_inc(rscored.sem, 1)

                def rapply(u):
                    _, i, c = units[u]
                    tk, w = CHUNKS[c]
                    sl = u % 2
                    eng.wait_ge(rdiag.sem, u + 1)
                    if c < len(CHUNKS) - 1:
                        eng.wait_ge(rrest.sem, rrest.at(*units[u]))
                    r0 = 64 * (i % 2)
                    spans = [(0, META), (META, T1)] if c == 0 else [(tk, T1)]
                    for lo, hi in spans:
                        at0 = (i // 2) * 1024 + 496
                        mm = eng.matmul(big[r0:r0 + 64, at0 + lo:at0 + hi],
                                        rvtok[0:w, c * 256 + i * RDV:c * 256 + (i + 1) * RDV],
                                        rp[0:w, sl * T1 + lo - tk:sl * T1 + hi - tk],
                                        start=c == 0, stop=(c == len(CHUNKS) - 1) or (c == 0 and lo == 0),
                                        skip_group_check=True)
                    mm.then_inc(rapplied.sem, 1)

                eng.wait_ge(rope_step.sem, rope_step.at(l, "k", 2))
                eng.wait_ge(rvtok_ready.sem, rvtok_ready.at(l))
                u0 = units.index((l, 0, 0))
                rscore(u0)
                for u in range(u0, u0 + 20):
                    if u + 1 < u0 + 20:
                        rscore(u + 1)
                    rapply(u)
                for p in range(2):
                    eng.wait_ge(ro_ready.sem, ro_ready.at(l, p))
                    spread(wide(misc, p, T1), square("mean64"), c1(ro, p), T1).then_inc(rmean.sem, 1)
                for p in range(2):
                    eng.wait_ge(rsq.sem, rsq.at(l, p))
                    mm = column_means(misc, 10 * p, "mean64", c1(rp, p), T1, heads=2)
                mm.then_inc(rvar.sem, 1)
                eng.wait_ge(rrstd.sem, rrstd.at(l))
                for p in range(2):
                    row_spread(misc, p, 10 * p, T1, heads=2).then_inc(rspread.sem, 1)
                first_pair(wout, t0 + MIX_TILES, T1, q0 + KD)
                repeat(eng, 1, KD // 2, lambda i: plain_pair(wout, t0 + MIX_TILES, i, T1))

            def attn(n, ph):
                win, wout = ph[2], ph[3]
                s0, t0, q0 = win.base, tile_of[n], fill_of[n]

                def ms(pair, s):
                    k = 2 * pair + s
                    eng.wait_ge(tile_out[s], t0 // 2 + pair + 1)
                    if not isinstance(k, int) or k >= 2:
                        eng.wait_ge(qrstd, k - 1)
                    spread(misc[:, s * 1024:s * 1024 + T2], square("mean64"), c1(sqr, s, T2), T2).then_inc(qms_done, 1)

                def one(i, s):
                    slab_ready(s0 + 2 * i + s)
                    slot_free(s, t0 // 2 + i)
                    slab(s, KD, xhigh, xlow, T2, s)
                first_pair(win, t0, T2, q0)
                ms(0, 0)

                def body(i):
                    one(i, 0)
                    ms(i - 1, 1)
                    one(i, 1)
                    ms(i, 0)
                body(1)
                repeat(eng, 2, 8, body)
                one(8, 0)
                ms(7, 1)
                one(8, 1)
                repeat(eng, 9, 12, lambda i: (one(i, 0), one(i, 1)))

                def score(u):
                    m, b = u // 4, u % 4
                    L = (b + 1) * P
                    sl = u % 2
                    if u >= 2:
                        eng.wait_ge(aexp_ready, u - 1)
                    for c in range(2):
                        rows = slice(64 * c, 64 * c + 64)
                        mm = eng.matmul(misc[:, sl * 1024 + c * 512:sl * 1024 + c * 512 + L],
                                        qkv[rows, m * T2 + b * P:m * T2 + (b + 1) * P],
                                        qkv[rows, (8 + m) * T2:(8 + m) * T2 + L], start=True, stop=True)
                    mm.then_inc(ascored, 1)

                def turn(k):
                    m, b = k // 5, k % 5
                    if k >= 2:
                        eng.wait_ge(atok_ready, k - 1)
                    if b:
                        eng.wait_ge(a_ready, 4 * m + b)
                    for j in range(b or 4):
                        src = c2(qkv, 16 + m, P, j * P) if b == 0 else c2(aa, (4 * m + b - 1) % 2, P, j * P)
                        mm = eng.transpose(big[:, (k % 2) * 512 + j * P:(k % 2) * 512 + (j + 1) * P], src, ident)
                    mm.then_inc(aturned, 1)

                def out_means(m):
                    eng.wait_ge(aosq, m + 1)
                    column_means(big, 1024 + (m % 2) * 512, "mean128", c1(sqr, m % 2, T2), T2).then_inc(aoms, 1)

                def out_spread(m):
                    eng.wait_ge(aorstd, m + 1)
                    row_spread(big[:, 1024 + (m % 2) * 512:1536 + (m % 2) * 512], 0, 0, T2).then_inc(aospread, 1)

                def apply(u):
                    m, b = u // 4, u % 4
                    eng.wait_ge(atok_ready, 5 * m + b + 2)
                    if b == 0 and m >= 2:
                        eng.wait_ge(fresh_ready, q0 + KD + m - 1)
                    o = big[:, 1024 + (m % 2) * 512 + b * P:1024 + (m % 2) * 512 + (b + 1) * P]
                    for j in range(b + 1):
                        mm = eng.matmul(o, c2(avt, m % 2, P, j * P), c2(at, u % 2, P, j * P),
                                        start=j == 0, stop=j == b)
                    mm.then_inc(aapplied, 1)

                eng.wait_ge(qn_ready, 16)
                for s in range(2):
                    eng.wait_ge(tile_out[s], (t0 + 24) // 2)
                turn(0)
                score(0)
                score(1)
                for u in range(32):
                    m, b = u // 4, u % 4
                    if b == 1 and m:
                        out_means(m - 1)
                    if b == 2 and m:
                        out_spread(m - 1)
                    if u + 2 < 32:
                        score(u + 2)
                    turn(5 * m + b + 1)
                    if b == 3 and m < 7:
                        turn(5 * (m + 1))
                    apply(u)
                out_means(7)
                out_spread(7)
                eng.wait_ge(fresh_ready, q0 + KD + 8)
                first_pair(wout, t0 + 24, T2, q0 + KD)
                repeat(eng, 1, KD // 2, lambda i: plain_pair(wout, t0 + 24, i, T2))

            def gmlp(n, ph):
                sv, su, so = ph[2:]
                t0, q0 = tile_of[n], fill_of[n]
                first_pair(sv, t0, T2, q0)
                eng.wait_ge(ws_in, 32)
                eng.wait_ge(rstd_wide, norm_of[n] + 1)
                for g in range(8):
                    if g >= 2:
                        eng.wait_ge(ws_ready, g - 1)
                    eng.transpose(misc[:, (g % 2) * 1024:(g % 2) * 1024 + P], wraw[:, g * P:(g + 1) * P], ident
                                  ).then_inc(ws_turned, 1)
                repeat(eng, 1, NG // 2, lambda i: plain_pair(sv, t0, i, T2))
                tu = t0 + NG
                plain_pair(su, tu, 0, T2)
                eng.wait_ge(g_sum, 1 + NG)
                eng.wait_ge(ws_ready, 8)
                spread(misc[:, 0:T2], square("mean1024"), acc, T2).then_inc(g_stat, 1)
                repeat(eng, 1, 5, lambda i: plain_pair(su, tu, i, T2))
                eng.wait_ge(g_sum, 2 * (1 + NG))
                spread(misc[:, 0:T2], square("mean1024"), acc, T2).then_inc(g_stat, 1)
                repeat(eng, 5, NG // 2, lambda i: plain_pair(su, tu, i, T2))

                def turn(m):
                    eng.wait_ge(g_affine, m + 1)
                    if m >= 2:
                        eng.wait_ge(g_tok, m - 1)
                    for j in range(4):
                        mm = eng.transpose(misc[:, (m % 2) * 1024 + j * P:(m % 2) * 1024 + (j + 1) * P],
                                           c2(vv, m, P, j * P), ident)
                    mm.then_inc(g_turned, 1)
                eng.wait_ge(g_statv, 2)
                turn(0)
                for m in range(NG):
                    if m + 1 < NG:
                        turn(m + 1)
                    eng.wait_ge(g_tok, m + 1)
                    if m >= 2:
                        eng.wait_ge(g_step, m - 1)
                    for j in range(4):
                        at0 = (m % 2) * 1024 + 512 + j * P
                        mm = eng.matmul(misc[:, at0:at0 + P], c1(vtm, m % 2, P, j * P),
                                        wt[:, (m // 2) * P:(m // 2 + 1) * P], start=True, stop=True)
                    mm.then_inc(g_mixed, 1)

                to = t0 + 2 * NG

                def two(i, before=None):
                    for s in range(2):
                        slot_free(s, to // 2 + i)
                        for half in range(2):
                            slab_ready(so.base + 4 * i + 2 * s + half)
                            slab(half, KD, xhigh if half == 0 else g2h, xlow if half == 0 else g2l, T2, s,
                                 width=T1 if half == 0 else T2, start=half == 0, stop=half == 1,
                                 before=before(half) if before and s == 0 else None)
                two(0, lambda half: operand(q0 + KD + half * KD))
                repeat(eng, 1, KD // 2, two)

            for n, ph in enumerate(plan):
                norm_sum(norm_of[n])
                if ph[0] != "final":
                    {"mix": mix, "cffn": ffn, "ffn": ffn, "attn": attn, "gmlp": gmlp}[ph[0]](n, ph)
            if plan[-1][0] == "final":
                eng.wait_ge(final_done, KD)
            else:
                for s in range(2):
                    eng.wait_ge(tile_out[s], tiles // 2)
            for tb in range(4):
                for half in range(2):
                    k = 2 * tb + half
                    if k >= 4:
                        eng.wait_ge(store_copied, k - 3)
                    for j in range(4):
                        mm = eng.transpose(misc[:, (k % 4) * 512 + j * P:(k % 4) * 512 + (j + 1) * P],
                                           h[:, (4 * half + j) * T1 + META + tb * P:(4 * half + j) * T1 + META + (tb + 1) * P],
                                           ident)
                    mm.then_inc(store_turned, 1)


def kernel(upto=99, **inputs):
    import concourse.bacc as bacc
    from concourse.bass_utils import run_bass_kernel_spmd

    nc = bacc.Bacc("TRN2", target_bir_lowering=False, num_devices=1)
    arrays, args = {}, {}
    for name, value in {**{k: np.ascontiguousarray(v) for k, v in inputs.items()}, **constants()}.items():
        arrays[f"in_{name}"] = value
        args[name] = nc.dram_tensor(f"in_{name}", value.shape, F32, kind="ExternalInput").ap()
    result = nc.dram_tensor("result", (SEQ, D), F32, kind="ExternalOutput").ap()
    build(nc, args, result, upto)
    r = run_bass_kernel_spmd(nc, [arrays], core_ids=[0])
    return r.results[0]["result"].reshape(1, SEQ, D)
```
